# Optimizing a Trainium2 kernel written in Bass

```python
import math
import jax, jax.numpy as jnp
from jax import lax
import numpy as np

D_MODEL = 1024
BATCH = 1
SEQ = 1024
DEPTH = 1

D_MIX = D_MODEL
D_ATTN = D_MIX // 2
D_CONV = D_MIX - D_ATTN
HEAD_DIM = 64
N_HEADS = D_ATTN // HEAD_DIM
CONV_GROUP = 64
N_CONV_GROUPS = D_CONV // CONV_GROUP
DILATED_CONFIGS = ((128, 1), (512, 4), (2048, 16))
BAND_BLOCK = 128
CONV_WIDTH = 3
FFN_CONV_WIDTH = 3
D_FF = 2816
EPS = 1e-6

kernel_name = "hybrid_dilated_attn_shortconv_convffn"

def rmsnorm(x, g):
    xf = x.astype(jnp.float32)
    y = xf * lax.rsqrt(jnp.mean(xf * xf, axis=-1, keepdims=True) + EPS)
    return (y * g.astype(jnp.float32)).astype(x.dtype)

def group_rmsnorm(x, g, n_groups):
    shp = x.shape
    xg = x.reshape(*shp[:-1], n_groups, shp[-1] // n_groups)
    return rmsnorm(xg, g.reshape(n_groups, -1)).reshape(shp)

def causal_dwconv(u, w):
    K = w.shape[0]
    S = u.shape[1]
    up = jnp.pad(u, ((0, 0), (K - 1, 0), (0, 0)))
    return sum(up[:, k:k + S] * w[k].astype(u.dtype) for k in range(K))

def alibi_slopes(n):
    return 2.0 ** (-8.0 * jnp.arange(1, n + 1, dtype=jnp.float32) / n)

def dilated_branch(q, k, v, slopes, window, dilation):
    B, H, S, hd = q.shape
    span = window // dilation
    L = S // dilation
    nb = -(-L // BAND_BLOCK)
    Lp = nb * BAND_BLOCK

    def to_blocks(t):
        t = t.reshape(B, H, L, dilation, hd).transpose(0, 1, 3, 2, 4)
        t = jnp.pad(t, ((0, 0), (0, 0), (0, 0), (0, Lp - L), (0, 0)))
        return t.reshape(B, H, dilation, nb, BAND_BLOCK, hd)

    def with_prev(t):
        prev = jnp.pad(t, ((0, 0), (0, 0), (0, 0), (1, 0), (0, 0), (0, 0)))[:, :, :, :-1]
        return jnp.concatenate([prev, t], axis=-2)

    qb, kb, vb = to_blocks(q), to_blocks(k), to_blocks(v)
    kk, vv = with_prev(kb), with_prev(vb)
    s = jnp.einsum('bhrnqd,bhrnkd->bhrnqk', qb, kk)
    i = jnp.arange(BAND_BLOCK)[:, None]
    j = jnp.arange(2 * BAND_BLOCK)[None, :]
    dist = BAND_BLOCK + i - j
    blk = jnp.arange(nb)[:, None, None]
    valid = (dist >= 0) & (dist <= span) & ((blk > 0) | (j >= BAND_BLOCK))
    bias = -(slopes * dilation).reshape(1, H, 1, 1, 1, 1) * dist.astype(jnp.float32)
    s = jnp.where(valid, s + bias, -jnp.inf)
    m = jnp.max(s, axis=-1)
    p = jnp.exp(s - m[..., None])
    l = jnp.sum(p, axis=-1)
    o = jnp.einsum('bhrnqk,bhrnkd->bhrnqd', p, vv)

    def from_blocks(t):
        rest = t.shape[5:]
        t = t.reshape(B, H, dilation, Lp, *rest)[:, :, :, :L]
        t = jnp.moveaxis(t, 2, 3)
        return t.reshape(B, H, S, *rest)

    return from_blocks(o), from_blocks(m), from_blocks(l)

def dilated_attention(q, k, v):
    slopes = alibi_slopes(q.shape[1])
    outs = [dilated_branch(q, k, v, slopes, w, d) for (w, d) in DILATED_CONFIGS]
    m_max = jnp.max(jnp.stack([m for (_, m, _) in outs]), axis=0)
    num = sum(o * jnp.exp(m - m_max)[..., None] for (o, m, _) in outs)
    den = sum(l * jnp.exp(m - m_max) for (_, m, l) in outs)
    return num / den[..., None]

def hybrid_mixer(h, w_in, mix_conv_w, attn_out_g, conv_out_g, w_out):
    B, S, _ = h.shape
    proj = h @ w_in
    q, k, v, gate_b, gate_c, u = jnp.split(
        proj, [D_ATTN, 2 * D_ATTN, 3 * D_ATTN, 3 * D_ATTN + D_CONV, 3 * D_ATTN + 2 * D_CONV], axis=-1)

    def heads(t):
        return t.reshape(B, S, N_HEADS, HEAD_DIM).transpose(0, 2, 1, 3).astype(jnp.float32)

    attn = dilated_attention(heads(q) * (HEAD_DIM ** -0.5), heads(k), heads(v))
    attn = attn.transpose(0, 2, 1, 3).reshape(B, S, D_ATTN).astype(h.dtype)
    attn = group_rmsnorm(attn, attn_out_g, N_HEADS)

    y = gate_b * causal_dwconv(gate_c * u, mix_conv_w)
    y = group_rmsnorm(y, conv_out_g, N_CONV_GROUPS)

    return jnp.concatenate([attn, y], axis=-1) @ w_out

def conv_glu_ffn(h, ffn_up, ffn_conv_w, ffn_down):
    up = causal_dwconv(h @ ffn_up, ffn_conv_w)
    gate, val = jnp.split(up, 2, axis=-1)
    return (jax.nn.silu(gate) * val) @ ffn_down

def setup_inputs(seed: int = 0) -> dict:
    key = jax.random.key(seed)
    ks = jax.random.split(key, 12)
    f32 = jnp.float32
    n = jax.random.normal
    d_in = 3 * D_ATTN + 3 * D_CONV
    return {
        "x": n(ks[0], (BATCH, SEQ, D_MODEL), f32),
        "norm1_g": 1.0 + 0.02 * n(ks[1], (DEPTH, D_MODEL), f32),
        "w_in": n(ks[2], (DEPTH, D_MODEL, d_in), f32) * D_MODEL ** -0.5,
        "mix_conv_w": n(ks[3], (DEPTH, CONV_WIDTH, D_CONV), f32) * CONV_WIDTH ** -0.5,
        "attn_out_g": 1.0 + 0.02 * n(ks[4], (DEPTH, D_ATTN), f32),
        "conv_out_g": 1.0 + 0.02 * n(ks[5], (DEPTH, D_CONV), f32),
        "w_out": n(ks[6], (DEPTH, D_MIX, D_MODEL), f32) * D_MIX ** -0.5,
        "norm2_g": 1.0 + 0.02 * n(ks[7], (DEPTH, D_MODEL), f32),
        "ffn_up": n(ks[8], (DEPTH, D_MODEL, 2 * D_FF), f32) * D_MODEL ** -0.5,
        "ffn_conv_w": n(ks[9], (DEPTH, FFN_CONV_WIDTH, 2 * D_FF), f32) * FFN_CONV_WIDTH ** -0.5,
        "ffn_down": n(ks[10], (DEPTH, D_FF, D_MODEL), f32) * D_FF ** -0.5,
        "final_norm_g": 1.0 + 0.02 * n(ks[11], (D_MODEL,), f32),
    }

def reference(x, norm1_g, w_in, mix_conv_w, attn_out_g, conv_out_g, w_out,
              norm2_g, ffn_up, ffn_conv_w, ffn_down, final_norm_g):
    for layer in range(DEPTH):
        h = rmsnorm(x, norm1_g[layer])
        x = x + hybrid_mixer(h, w_in[layer], mix_conv_w[layer], attn_out_g[layer],
                             conv_out_g[layer], w_out[layer])
        h = rmsnorm(x, norm2_g[layer])
        x = x + conv_glu_ffn(h, ffn_up[layer], ffn_conv_w[layer], ffn_down[layer])
    return rmsnorm(x, final_norm_g)


_drawn_inputs = setup_inputs


def setup_inputs(seed=0):
    import zlib

    import numpy as np

    out = dict(_drawn_inputs(seed))
    spreads = {}
    factors = {'attn_out_g': 5.34, 'conv_out_g': 5.09, 'norm2_g': 5.042, 'final_norm_g': 2.83}
    for name, (base, spread) in spreads.items():
        noise = np.random.default_rng([zlib.crc32(name.encode()), seed]).standard_normal(out[name].shape)
        drawn = base * np.exp(spread * noise) if base else spread * noise
        out[name] = __import__('jax').numpy.asarray(drawn.astype(out[name].dtype))
    for name, factor in factors.items():
        out[name] = (out[name] * factor).astype(out[name].dtype)
    return out
```

```python
from contextlib import ExitStack

import concourse.bass as bass
from concourse import mybir

F32 = mybir.dt.float32
F32R = mybir.dt.float32r
ALU = mybir.AluOpType
ACT = mybir.ActivationFunctionType
AX = mybir.AxisListType

P = 128
EPS = 1e-6
MASKED = -1e30


class Ring:

    def __init__(self, depth, turns, rest):
        self.depth, self.turns, self.rest = depth, turns, rest

    def n(self, k):
        return self.turns * self.depth + (self.rest + k)

    def slot(self, k):
        return (self.rest + k) % self.depth

    def turn(self, k):
        return self.turns + (self.rest + k) // self.depth


def mixer_tiles(kind):
    if kind == "first":
        return ["q", "k", "v", "c", "u", "b"]
    if kind == "last":
        return ["oA", "oC"]
    return ["q", "k", "v", "oA", "oC", "c", "u", "b"]


def ffn_tiles(kind):
    if kind == "first":
        return ["g0", "v0", "g1", "v1"]
    if kind == "last":
        return ["dA", "dB"]
    return ["g0", "dA", "dB", "v0", "g1", "v1"]


def proj(tile, half):
    return [("proj", tile, half, c) for c in range(4)]


def mixer_steps(kind, NT):
    tiles = mixer_tiles(kind)
    at = {t: i for i, t in enumerate(tiles)}
    steps = []
    if kind != "last":
        steps += proj("q", 0) + proj("q", 1) + [("split", at["q"] + 2)]
    chunks = proj("k", 0) + proj("k", 1) if kind != "last" else [None] * 8
    tail = {1: [("attT", 0)], 3: [("attT", 1)], 5: [("stat", 0)], 7: [("stat", 1), ("yhi", 0), ("yhi", 1)]}
    for n, c in enumerate(chunks):
        steps += [c] if c else []
        steps += tail.get(n, []) if kind != "first" else []
    if kind != "last":
        steps.append(("split", at["k"] + 2))
    outs = [("out", b) for b in range(2 * NT)]
    if kind == "last":
        for b in outs:
            steps.append(b)
            t = b[1] // 2
            if b[1] % 2 == 1:
                steps.append(("square", t))
            else:
                if t >= 1:
                    steps += [("scale", t - 1)]
                if t >= 2:
                    steps += [("nT", t - 2, 0), ("nT", t - 2, 1)]
        steps += [("scale", NT - 1)]
        for t in (NT - 2, NT - 1):
            steps += [("nT", t, 0), ("nT", t, 1)]
        return steps
    steps += proj("v", 0) + proj("v", 1) + [("split", at["v"] + 2)]
    fill = []
    if kind != "first":
        fill += [[b] for b in outs]
        fill[-1] += [("split", at["oA"] + 2), ("split", at["oC"] + 2)]
    for x in "cub":
        chunks = proj(x, 0) + proj(x, 1)
        fill += [[c] for c in chunks]
        fill[-1].append(("split", at[x] + 2))

    def F(n=1):
        for _ in range(n):
            if fill:
                steps.extend(fill.pop(0))

    groups = [(hd, g) for hd in range(2) for g in range(NT // 2)]
    steps += [("qk", 0, 0), ("vT", 0), ("vT", 1), ("qk", 0, 1)]
    F(1)
    for n, (hd, g) in enumerate(groups):
        after = groups[n + 1] if n + 1 < len(groups) else None
        for p in range(g + 1):
            steps.append(("tp", hd, g, p))
            F()
            if p == 0 and g == 0 and hd == 1:
                steps += [("otok", 0), ("oroot", 0)]
            if p == 0 and g == 1 and hd == 1:
                steps.append(("oscale", 0))
            if p >= 1:
                steps.append(("pv", hd, g, p - 1))
        if after:
            steps.append(("qk", after[0], 2 * after[1]))
            F()
        steps.append(("pv", hd, g, g))
        if after:
            steps.append(("qk", after[0], 2 * after[1] + 1))
            F(2 if g < 2 else 1)
    F(2)
    steps += [("otok", 1), ("oroot", 1)]
    F()
    steps.append(("oscale", 1))
    while fill:
        F()
    return steps


def ffn_steps(kind, NT):
    tiles = ffn_tiles(kind)
    at = {t: i for i, t in enumerate(tiles)}
    downs = [("down", b) for b in range(2 * NT)]
    if kind == "last":
        steps = []
        for d in downs:
            steps.append(d)
            t = d[1] // 2
            if d[1] % 2 == 1:
                steps.append(("square", t))
            elif t >= 1:
                steps.append(("finish", t - 1))
        return steps + [("finish", NT - 1)]
    steps = [] if kind == "first" else [("split", 2)]
    for a in range(2):
        steps += [("up", "g", a, 0), ("up", "g", a, 1), ("split", at[f"g{a}"] + 3)]
        if a == 0 and kind != "first":
            steps += downs + [("split", at["dA"] + 3), ("split", at["dB"] + 3)]
        steps += [("silu", a, 0), ("silu", a, 1)]
        steps += [("up", "v", a, 0), ("prod", a, 0), ("up", "v", a, 1), ("prod", a, 1)]
        if a == 0:
            steps += [("split", at["v0"] + 3)]
    return steps


def numbered(steps, kinds):
    out = {}
    for s in steps:
        if s[0] in kinds and (s[0] != "proj" or s[3] == 3):
            out[s[:3] if s[0] == "proj" else s] = len(out)
    return out


def reg_slot(s):
    _, hd, g, p = s
    return (hd * 6 + g * (g - 1) // 2 + p) % 2


def last_user(s, pvs):
    _, hd, g, p = s
    if p == g:
        return None
    order = [q for q in pvs if q[3] < q[2]]
    at = order.index(("pv", hd, g, p))
    return pvs[order[at - 2]] if at >= 2 else None


def chained(steps, NT):
    per = {"qk": 1, "otok": 2}
    n = sum(per.get(s[0], 0) for s in steps)
    n += sum(s[0] == "qk" and s[2] == NT - 1 for s in steps)
    return n + 2 * sum(s[:3] == ("proj", "b", 0) and s[3] == 3 for s in steps)


ACC_KINDS = ("proj", "out", "nT", "up", "down")
TURN_KINDS = ("vT", "tp", "otok", "attT", "stat")
TURN_HI_KINDS = ("vT", "tp", "attT")


def build_program(nc, x, norm1_g, w_in, mix_conv_w, attn_out_g, conv_out_g, w_out, norm2_g, ffn_up,
                  ffn_conv_w, ffn_down, final_norm_g, bias_table, log_counts, out):
    _, S, D = x.shape
    NT = S // P
    KT = D // P
    HALF = S // 2
    HT = NT // 2
    HD = 64
    D_ATTN = attn_out_g.shape[1]
    NJ = D_ATTN // P
    F = ffn_down.shape[1]
    FTILES = F // P
    NI = FTILES // 2
    assert D == 2 * D_ATTN and S == 1024 and FTILES % 2 == 0 and KT == 8

    MIX = {k: mixer_steps(k, NT) for k in ("first", "loop", "last")}
    FFN = {k: ffn_steps(k, NT) for k in ("first", "loop", "last")}

    def total(steps, kinds):
        return len(numbered(steps, kinds))

    def mixer_base(kinds, j, before=0):
        if isinstance(j, int) and j == 0:
            return before
        first, loop = total(MIX["first"], kinds), total(MIX["loop"], kinds)
        return j * loop + (before + first - loop)

    def ffn_base(kinds, i, before=0):
        if isinstance(i, int) and i == 0:
            return before
        first, loop = total(FFN["first"], kinds), total(FFN["loop"], kinds)
        return i * loop + (before + first - loop)

    NORM1_ACC = 2 * NT
    MIX_ACC = mixer_base(ACC_KINDS, NJ, NORM1_ACC) + total(MIX["last"], ACC_KINDS)
    MIX_HI = 2 * NT + 4 * NJ + 2 * NT
    NACC = 4
    assert NORM1_ACC % NACC == 0 and MIX_ACC % NACC == 0
    assert mixer_base(ACC_KINDS, 1, NORM1_ACC) % NACC == 0
    assert mixer_base(ACC_KINDS, 2) % NACC == mixer_base(ACC_KINDS, 1) % NACC
    assert ffn_base(ACC_KINDS, 1) % NACC == 0 and ffn_base(ACC_KINDS, 2) % NACC == 0

    def mixer_ring(j):
        return Ring(2, 0, 0) if isinstance(j, int) and j == 0 else Ring(2, j * 4 - 1, 0)

    def ffn_ring(i):
        return Ring(3, 0, 0) if isinstance(i, int) and i == 0 else Ring(3, i * 2 - 1, 1)

    ctx = ExitStack()
    with ctx:
        def sb(name, shape, dt=F32, scope=ctx):
            return scope.enter_context(nc.sbuf_tensor(name, shape, dt))

        def sem(name):
            return ctx.enter_context(nc.semaphore(name))

        h_hi = sb("h_hi", [P, KT, S], F32R)
        h_lo = sb("h_lo", [P, KT, S], F32R)
        res = sb("res", [P, NT, D])
        ident = sb("ident", [P, P])
        fold = sb("fold", [P, HD])
        mean64 = sb("mean64", [P, P])
        params = sb("params", [P, 3 * 2 * FTILES + 5 * NJ])
        ss = sb("ss", [P, NT])
        rstd = sb("rstd", [P, NT])
        eps = sb("eps", [P, 1])
        now = sb("now", [P, 5])
        NCW = 3 * 2 * FTILES
        ffn_w = params[:, 0:NCW].rearrange("p (k t) -> p k t", k=3)
        mix_w = params[:, NCW:NCW + 3 * NJ].rearrange("p (k t) -> p k t", k=3)
        attn_g = params[:, NCW + 3 * NJ:NCW + 4 * NJ]
        conv_g = params[:, NCW + 4 * NJ:NCW + 5 * NJ]

        with ExitStack() as scope:
            hn1 = sb("hn1", [P, 2, D], F32, scope)
            g1_row = sb("g1_row", [P, D], F32, scope)
            param_rows = sb("param_rows", [P, 8, P], F32, scope)
        with ExitStack() as scope:
            mixA_hi = sb("mixA_hi", [P, S], F32R, scope)
            mixA_lo = sb("mixA_lo", [P, S], F32R, scope)
            mixC_hi = sb("mixC_hi", [P, S], F32R, scope)
            mixC_lo = sb("mixC_lo", [P, S], F32R, scope)
            Q = [sb(f"Q{n}", [P, S], F32R, scope) for n in range(2)]
            K1 = [sb(f"K1_{n}", [P, S], F32R, scope) for n in range(2)]
            K2 = [sb(f"K2_{n}", [P, S], F32R, scope) for n in range(2)]
            V = sb("V", [P, NT, 2, P], F32R, scope)
            probT_hi = sb("probT_hi", [P, 2, 2, 256], F32R, scope)
            probT_lo = sb("probT_lo", [P, 2, 2, 256], F32R, scope)
            diagT_hi = sb("diagT_hi", [P, 2, 256], F32R, scope)
            diagT_lo = sb("diagT_lo", [P, 2, 256], F32R, scope)
            prob = sb("prob", [P, 2, S], F32, scope)
            bias = sb("bias", [P, S], F32, scope)
            half_log = sb("half_log", [P, S], F32, scope)
            o_sb = sb("o_sb", [P, S], F32, scope)
            o_tok = sb("o_tok", [P, NT, HD], F32, scope)
            o_sq = sb("o_sq", [P, NT, HD], F32, scope)
            m_raw = sb("m_raw", [P, 2], F32, scope)
            marker = sb("marker", [P, 1], F32, scope)
            m_neg = sb("m_neg", [P, 2], F32, scope)
            l_sum = sb("l_sum", [P, 2, NT], F32, scope)
            l_inv = sb("l_inv", [P, NT], F32, scope)
            o_ss = sb("o_ss", [P, NT], F32, scope)
            o_r = sb("o_r", [P, NT], F32, scope)
            wraw = sb("wraw", [P, 2, 1024], F32, scope)
            whi = sb("whi", [P, 2, 1024], F32R, scope)
            wlo = sb("wlo", [P, 2, 1024], F32R, scope)
            att = sb("att", [P, NT, P], F32, scope)
            cu = sb("cu", [P, 2 + S], F32, scope)
            y = sb("y", [P, S], F32, scope)
        with ExitStack() as scope:
            a_hi = sb("a_hi", [P, 2, S], F32R, scope)
            a_lo = sb("a_lo", [P, 2, S], F32R, scope)
            fraw = sb("fraw", [P, 3, 1024], F32, scope)
            g2_row = sb("g2_row", [P, D], F32, scope)
            gf_row = sb("gf_row", [P, D], F32, scope)
            hn2 = sb("hn2", [P, 2, D], F32, scope)
            fhi = sb("fhi", [P, 3, 1024], F32R, scope)
            flo = sb("flo", [P, 3, 1024], F32R, scope)
            ub = {n: sb(f"ub_{n}", [P, 2 + S], F32, scope) for n in "gv"}
            z = {n: sb(f"z_{n}", [P, S], F32, scope) for n in "gv"}

        acc = [ctx.enter_context(nc.psum_tensor(f"acc{n}", [P, 512], F32)) for n in range(NACC)]
        turn = ctx.enter_context(nc.psum_tensor("turn", [P, 512], F32))
        score = ctx.enter_context(nc.psum_tensor("score", [P, 1024], F32))
        pv_out = ctx.enter_context(nc.psum_tensor("pv_out", [P, 512], F32))

        x_in = [sem(f"x_in{t}") for t in range(NT)]
        tables_in = sem("tables_in")
        rows_in = sem("rows_in")
        g1_in, g2_in, gf_in = sem("g1_in"), sem("g2_in"), sem("gf_in")
        w_in_slot = [sem(f"w_in_slot{n}") for n in range(2)]
        f_in_slot = [sem(f"f_in_slot{n}") for n in range(3)]
        consts = sem("consts")
        dconsts = sem("dconsts")
        params_turned = sem("params_turned")
        params_ready = sem("params_ready")
        w_hi_made, w_made = sem("w_hi_made"), sem("w_made")
        f_hi_made, f_made = sem("f_hi_made"), sem("f_made")
        squared = sem("squared")
        squared_log = sem("squared_log")
        rstd_ready = sem("rstd_ready")
        o_ss_ready = sem("o_ss_ready")
        o_log, o_r_ready = sem("o_log"), sem("o_r_ready")
        y_log, y_r_ready = sem("y_log"), sem("y_r_ready")
        scaled = sem("scaled")
        acc_full, acc_drained = sem("acc_full"), sem("acc_drained")
        acc_hi = sem("acc_hi")
        turn_full, turn_drained, turn_hi = sem("turn_full"), sem("turn_drained"), sem("turn_hi")
        score_full = sem("score_full")
        logits_ready = sem("logits_ready")
        probs_ready = sem("probs_ready")
        pv_done = sem("pv_done")
        o_copied = sem("o_copied")
        att_ready = sem("att_ready")
        tap_ready = sem("tap_ready")
        now_ready = sem("now_ready")
        y_squared, y_hi, y_lo = sem("y_squared"), sem("y_hi"), sem("y_lo")
        pads = sem("pads")
        u_ready = sem("u_ready")
        silu_done, prod_done, a_hi_done, a_lo_done = sem("silu_done"), sem("prod_done"), sem("a_hi_done"), sem("a_lo_done")
        dve_chain = sem("dve_chain")
        stored = [sem(f"stored{n}") for n in range(2)]

        x_d = x[0].rearrange("(t p) d -> t p d", p=P)
        out_d = out[0].rearrange("(t p) d -> t p d", p=P)
        w_in_d = w_in[0].rearrange("(k p) c -> p k c", p=P)
        up_d = ffn_up[0].rearrange("(k p) c -> p k c", p=P)
        IN_AT = {"q": 0, "k": D_ATTN, "v": 2 * D_ATTN, "b": 3 * D_ATTN, "c": 3 * D_ATTN + D_ATTN, "u": 5 * D_ATTN}

        def half(t, n):
            return t[:, n * HALF:(n + 1) * HALF]

        def keys_of(qb):
            n = P * (qb + 1)
            pieces = [(0, min(max(n, 256), 512))]
            if n > 512:
                pieces.append((512, max(n - 512, 256)))
            return pieces

        block = ctx.enter_context(nc.Block())

        @block.sync
        def _(sp):
            def mixer_weights(kind, j, ks):
                ring = mixer_ring(j)
                for k in ks:
                    tile = mixer_tiles(kind)[k]
                    if not (kind == "first" and k < 2):
                        sp.wait_ge(w_made, ring.n(k) - 1)
                    dst = wraw[:, ring.slot(k), :]
                    if tile[0] == "o":
                        row = (j - 1) * P + (0 if tile == "oA" else D_ATTN)
                        src = w_out[0][bass.ds(row, P), :]
                    else:
                        src = w_in_d[:, :, bass.ds(j * P + IN_AT[tile], P)]
                        dst = dst.rearrange("p (k c) -> p k c", k=KT)
                    sp.dma_start(dst, src).then_inc(w_in_slot[ring.slot(k)], 16)

            def ffn_weights(kind, i):
                ring = ffn_ring(i)
                for k, tile in enumerate(ffn_tiles(kind)):
                    if not (kind == "first" and k < 3):
                        sp.wait_ge(f_made, ring.n(k) - 2)
                    dst = fraw[:, ring.slot(k), :]
                    if tile[0] == "d":
                        row = (i - 1) * (2 * P) + (0 if tile == "dA" else P)
                        src = ffn_down[0][bass.ds(row, P), :]
                    else:
                        col = i * (2 * P) + (int(tile[1]) * P + (F if tile[0] == "v" else 0))
                        src = up_d[:, :, bass.ds(col, P)]
                        dst = dst.rearrange("p (k c) -> p k c", k=KT)
                    sp.dma_start(dst, src).then_inc(f_in_slot[ring.slot(k)], 16)

            sp.dma_start(res[:, 0, :], x_d[0]).then_inc(x_in[0], 16)
            sp.dma_start(g1_row[:], norm1_g[0].partition_broadcast(P)).then_inc(g1_in, 16)
            for t in range(1, HT):
                sp.dma_start(res[:, t, :], x_d[t]).then_inc(x_in[t], 16)
            sp.dma_start(param_rows[0:2 * FTILES, 0:3, :],
                         ffn_conv_w[0].rearrange("k (t p) -> t k p", p=P)).then_inc(rows_in, 16)
            sp.dma_start(param_rows[0:NJ, 3:6, :],
                         mix_conv_w[0].rearrange("k (t p) -> t k p", p=P)).then_inc(rows_in, 16)
            sp.dma_start(param_rows[0:NJ, 6, :], attn_out_g[0].rearrange("(t p) -> t p", p=P)).then_inc(rows_in, 16)
            sp.dma_start(param_rows[0:NJ, 7, :], conv_out_g[0].rearrange("(t p) -> t p", p=P)).then_inc(rows_in, 16)
            mixer_weights("first", 0, range(2))
            for t in range(HT, NT):
                sp.dma_start(res[:, t, :], x_d[t]).then_inc(x_in[t], 16)
            sp.dma_start(bias[:], bias_table).then_inc(tables_in, 16)
            sp.dma_start(half_log[:], log_counts).then_inc(tables_in, 16)
            mixer_weights("first", 0, range(2, 6))
            with sp.Fori(1, NJ) as j:
                mixer_weights("loop", j, range(8))
            mixer_weights("last", NJ, range(2))
            sp.wait_ge(score_full, 2 * NT * NJ)
            sp.dma_start(g2_row[:], norm2_g[0].partition_broadcast(P)).then_inc(g2_in, 16)
            ffn_weights("first", 0)
            sp.dma_start(gf_row[:], final_norm_g.partition_broadcast(P)).then_inc(gf_in, 16)
            with sp.Fori(1, NI) as i:
                ffn_weights("loop", i)
            ffn_weights("last", NI)
            for t in range(NT):
                sp.wait_ge(scaled, 2 * NT + t + 1)
                sp.dma_start(out_d[t], hn2[:, t % 2, :]).then_inc(stored[t % 2], 16)
            for s in stored:
                sp.wait_ge(s, 16 * (NT // 2))

        @block.gpsimd
        def _(pool):
            pool.memset(ident[:], 0.0).then_inc(consts, 1)
            pool.wait_ge(consts, 1)
            pool.affine_select(out=ident[:], in_=ident[:], compare_op=ALU.not_equal, fill=1.0, base=0,
                               pattern=[[-1, P]], channel_multiplier=1).then_inc(consts, 1)
            pool.wait_ge(consts, 2)
            pool.memset(eps[:], EPS).then_inc(consts, 1)
            pool.wait_ge(consts, 3)
            pool.memset(mean64[:], 0.0).then_inc(consts, 1)
            pool.wait_ge(consts, 4)
            pool.memset(mean64[0:HD, 0:HD], 1.0 / HD).then_inc(consts, 1)
            pool.wait_ge(consts, 5)
            pool.memset(mean64[HD:P, HD:P], 1.0 / HD).then_inc(consts, 1)
            pool.wait_ge(consts, 6)
            pool.memset(cu[:, 0:2], 0.0).then_inc(consts, 1)
            pool.wait_ge(consts, 7)
            pool.memset(diagT_hi[:, 1, 0:P].bitcast(F32), 0.0).then_inc(consts, 1)
            pool.wait_ge(consts, 8)
            pool.memset(diagT_lo[:, 1, 0:P].bitcast(F32), 0.0).then_inc(consts, 1)

        @block.scalar
        def _(act):
            def split_mixer(ring, k):
                act.wait_ge(w_in_slot[ring.slot(k)], (ring.turn(k) + 1) * 16)
                act.activation(whi[:, ring.slot(k), :], wraw[:, ring.slot(k), :], ACT.Copy).then_inc(w_hi_made, 1)

            def split_ffn(ring, k):
                act.wait_ge(f_in_slot[ring.slot(k)], (ring.turn(k) + 1) * 16)
                act.activation(fhi[:, ring.slot(k), :], fraw[:, ring.slot(k), :], ACT.Copy).then_inc(f_hi_made, 1)

            def square(t, hn, before):
                act.activation(hn[:, t % 2, :], res[:, t, :], ACT.Square, scale=float(D) ** -0.5,
                               accum_out=ss[:, t:t + 1]).then_inc(squared, 1)
                act.wait_ge(squared, before + t + 1)
                rsqrt(rstd[:, t:t + 1], ss[:, t:t + 1], squared_log, before + t + 1, rstd_ready)

            def rsqrt(dst, src, logged, n, ready):
                act.activation(dst, src, ACT.Ln, bias=eps[:, 0:1]).then_inc(logged, 1)
                act.wait_ge(logged, n)
                act.activation(dst, dst, ACT.Exp, scale=-0.5).then_inc(ready, 1)

            def norm_hi(bank, t, c):
                act.activation(h_hi[:, 4 * c:4 * c + 4, t * P:(t + 1) * P],
                               acc[bank][:, :].rearrange("p (k c) -> p k c", k=4), ACT.Copy).then_inc(acc_hi, 1)

            act.preload_act_table_set("natural_log_exp_and_others")
            act.wait_ge(consts, 3)
            for t in range(NT + 1):
                if t < NT:
                    act.wait_ge(x_in[t], 16)
                    if t >= 2:
                        act.wait_ge(acc_full, 2 * (t - 1))
                    square(t, hn1, 0)
                if t >= 1:
                    for c in range(2):
                        n = 2 * (t - 1) + c
                        act.wait_ge(acc_full, n + 1)
                        norm_hi(n % NACC, t - 1, c)
                if t in (HT, HT + 1):
                    split_mixer(mixer_ring(0), t - HT)
            act.wait_ge(params_ready, 1)
            act.wait_ge(consts, 7)

            def mixer(kind, j):
                steps = MIX[kind]
                ring = mixer_ring(j)
                accs, turns = numbered(steps, ACC_KINDS), numbered(steps, TURN_KINDS)
                acc0, turn0 = mixer_base(ACC_KINDS, j, NORM1_ACC), mixer_base(TURN_KINDS, j)
                scores = numbered(steps, ("qk",))
                pvs = numbered(steps, ("pv",))
                for s in steps:
                    if s[0] == "split":
                        k = s[1]
                        if kind == "last":
                            continue
                        before = mixer_tiles(kind)[k - 2]
                        use = ("out", 2 * NT - 1) if before[0] == "o" else ("proj", before, 1)
                        act.wait_ge(acc_full, acc0 + (accs[use] + 1))
                        split_mixer(ring, k)
                    elif s[0] == "proj" and s[3] == 3 and s[1] in "qk":
                        n = accs[s[:3]]
                        p, cols = acc[n % NACC], slice(s[2] * HALF, (s[2] + 1) * HALF)
                        act.wait_ge(acc_full, acc0 + (n + 1))
                        lo, up = slice(0, HD), slice(HD, P)
                        if s[1] == "q":
                            act.activation(Q[0][lo, cols], p[lo, :], ACT.Copy, scale=HD ** -0.5)
                            act.activation(Q[1][up, cols], p[up, :], ACT.Copy, scale=HD ** -0.5).then_inc(acc_hi, 1)
                        else:
                            act.activation(K1[0][lo, cols], p[lo, :], ACT.Copy)
                            act.activation(K2[0][up, cols], p[lo, :], ACT.Copy)
                            act.activation(K2[1][lo, cols], p[up, :], ACT.Copy)
                            act.activation(K1[1][up, cols], p[up, :], ACT.Copy).then_inc(acc_hi, 1)
                    elif s[0] == "proj" and s[3] == 3 and s[1:3] == ("u", 1):
                        act.wait_ge(acc_drained, acc0 + (accs[s[:3]] + 1))
                        act.activation(y[:, :], cu[:, 2:2 + S], ACT.Copy,
                                       scale=now[:, 2:3]).then_inc(tap_ready, 1)
                    elif s[0] == "proj" and s[3] == 3 and s[1:3] == ("b", 1):
                        act.wait_ge(acc_drained, acc0 + (accs[s[:3]] + 1))
                        act.activation(cu[:, 2:2 + S], y[:, :], ACT.Square).then_inc(y_squared, 1)
                    elif s[0] == "vT":
                        n = turns[s]
                        act.wait_ge(turn_full, turn0 + (n + 1))
                        src = turn[:, :].rearrange("p (t h d) -> p t h d", t=HT, h=2)
                        act.activation(V[:, HT * s[1]:HT * s[1] + HT, :, 0:HD], src, ACT.Copy).then_inc(turn_hi, 1)
                    elif s[0] == "attT":
                        n = turns[s]
                        act.wait_ge(now_ready, j + 1)
                        act.wait_ge(turn_full, turn0 + (n + 1))
                        act.activation(half(mixA_hi, s[1]), turn[:, :], ACT.Copy,
                                       scale=now[:, 3:4]).then_inc(turn_hi, 1)
                    elif s[0] == "stat":
                        n = (j - 1) * 2 + (s[1] + 1)
                        act.wait_ge(turn_full, turn0 + (turns[s] + 1))
                        rsqrt(cu[:, 2 + s[1] * HALF:2 + (s[1] + 1) * HALF], turn[:, :], y_log, n, y_r_ready)
                    elif s[0] == "yhi":
                        act.wait_ge(turn_drained, turn0 + (turns[("stat", s[1])] + 1))
                        act.activation(half(mixC_hi, s[1]), half(y, s[1]), ACT.Copy).then_inc(y_hi, 1)
                    elif s[0] == "qk":
                        _, hd, qb = s
                        act.wait_ge(logits_ready, j * (2 * NT) + (scores[s] + 1))
                        n = P * (qb + 1)
                        act.activation(prob[:, qb % 2, 0:n], prob[:, qb % 2, 0:n], ACT.Exp, bias=m_neg[:, qb % 2:qb % 2 + 1],
                                       accum_out=l_sum[:, hd, qb:qb + 1]).then_inc(probs_ready, 1)
                    elif s[0] == "tp":
                        _, hd, g, p = s
                        n = turns[s]
                        slot_free = last_user(s, pvs)
                        if slot_free is not None:
                            act.wait_ge(pv_done, j * len(pvs) + (slot_free + 1))
                        act.wait_ge(turn_full, turn0 + (n + 1))
                        src = turn[:, :].rearrange("p (k q) -> p k q", k=2)
                        if p < g:
                            act.activation(probT_hi[:, reg_slot(s), :, :], src, ACT.Copy).then_inc(turn_hi, 1)
                        else:
                            act.activation(diagT_hi[:, 0, :], src[:, 0, :], ACT.Copy)
                            act.activation(diagT_hi[:, 1, P:256], src[:, 1, P:256], ACT.Copy).then_inc(turn_hi, 1)
                    elif s[0] == "pv" and s[2] == s[3]:
                        g = s[2]
                        act.wait_ge(pv_done, j * len(pvs) + (pvs[s] + 1))
                        act.activation(o_sb[:, 256 * g:256 * g + 256], pv_out[:, 0:256], ACT.Copy).then_inc(o_copied, 1)
                    elif s[0] == "oroot":
                        act.wait_ge(o_ss_ready, j * 2 + (s[1] + 1))
                        rsqrt(o_r[:, :], o_ss[:, :], o_log, j * 2 + (s[1] + 1), o_r_ready)
                    elif s[0] == "square":
                        t = s[1]
                        act.wait_ge(acc_drained, acc0 + (accs[("out", 2 * t + 1)] + 1))
                        if t >= 2:
                            act.wait_ge(acc_full, acc0 + (accs[("nT", t - 2, 1)] + 1))
                        square(t, hn2, NT)
                    elif s[0] == "nT":
                        n = accs[s]
                        act.wait_ge(acc_full, acc0 + (n + 1))
                        norm_hi(n % NACC, s[1], s[2])
                    if s == ("attT", 1) and kind == "last":
                        for k in range(3):
                            split_ffn(ffn_ring(0), k)

            mixer("first", 0)
            with act.Fori(1, NJ) as j:
                mixer("loop", j)
            mixer("last", NJ)

            def ffn(kind, i):
                steps = FFN[kind]
                ring = ffn_ring(i)
                accs = numbered(steps, ACC_KINDS)
                acc0 = ffn_base(ACC_KINDS, i, MIX_ACC)
                for s in steps:
                    if s[0] == "split":
                        done = 0
                        if s[1] >= 3:
                            before = ffn_tiles(kind)[s[1] - 3]
                            use = ("down", 2 * NT - 1) if before[0] == "d" else ("up", before[0], int(before[1]), 1)
                            done = accs[use] + 1
                        act.wait_ge(acc_full, acc0 + done)
                        split_ffn(ring, s[1])
                    elif s[0] == "up":
                        _, what, a, hf = s
                        n = accs[s]
                        col = i * 2 + (a + (FTILES if what == "v" else 0))
                        act.wait_ge(acc_full, acc0 + (n + 1))
                        if hf == 0 and not (kind == "first" and a == 0):
                            act.wait_ge(a_lo_done, i * 4 + 2 * a)
                        act.activation(ub[what][:, 2 + hf * HALF:2 + (hf + 1) * HALF], acc[n % NACC][:, :], ACT.Copy)
                        act.activation(half(z[what], hf), acc[n % NACC][:, :], ACT.Copy,
                                       scale=ffn_w[:, 2, bass.ds(col, 1)]).then_inc(u_ready, 1)
                    elif s[0] == "silu":
                        _, a, hf = s
                        act.wait_ge(acc_drained, acc0 + (accs[("up", "g", a, hf)] + 1))
                        act.activation(half(z["g"], hf), half(z["g"], hf), ACT.Silu).then_inc(silu_done, 1)
                    elif s[0] == "prod":
                        _, a, hf = s
                        act.wait_ge(prod_done, i * 4 + (2 * a + hf + 1))
                        act.activation(half(a_hi[:, a, :], hf), half(z["g"], hf), ACT.Copy).then_inc(a_hi_done, 1)
                    elif s[0] == "square":
                        t = s[1]
                        act.wait_ge(acc_drained, acc0 + (accs[("down", 2 * t + 1)] + 1))
                        if t >= 2:
                            act.wait_ge(stored[t % 2], 16 * (t // 2))
                        square(t, hn2, 2 * NT)

            ffn("first", 0)
            with act.Fori(1, NI) as i:
                ffn("loop", i)
            act.preload_act_table_set("natural_log_exp_and_others")
            ffn("last", NI)

        @block.vector
        def _(dve):
            chain = {"base": 0, "n": 0}

            def then_chain(ins):
                chain["n"] += 1
                ins.then_inc(dve_chain, 1)
                dve.wait_ge(dve_chain, chain["base"] + chain["n"])

            def split_mixer(ring, k):
                dve.wait_ge(w_hi_made, ring.n(k) + 1)
                dve.tensor_tensor(wlo[:, ring.slot(k), :], wraw[:, ring.slot(k), :],
                                  whi[:, ring.slot(k), :].bitcast(F32), ALU.subtract).then_inc(w_made, 1)

            def split_ffn(ring, k):
                dve.wait_ge(f_hi_made, ring.n(k) + 1)
                dve.tensor_tensor(flo[:, ring.slot(k), :], fraw[:, ring.slot(k), :],
                                  fhi[:, ring.slot(k), :].bitcast(F32), ALU.subtract).then_inc(f_made, 1)

            def scale(t, hn, row, before):
                dve.wait_ge(rstd_ready, before + t + 1)
                dve.scalar_tensor_tensor(out=hn[:, t % 2, :], in0=res[:, t, :], scalar=rstd[:, t:t + 1],
                                         in1=row[:, :], op0=ALU.mult, op1=ALU.mult).then_inc(scaled, 1)

            def norm_lo(bank, t, c):
                cols = slice(t * P, (t + 1) * P)
                dve.tensor_tensor(h_lo[:, 4 * c:4 * c + 4, cols], acc[bank][:, :].rearrange("p (k c) -> p k c", k=4),
                                  h_hi[:, 4 * c:4 * c + 4, cols].bitcast(F32), ALU.subtract).then_inc(acc_drained, 1)

            dve.wait_ge(consts, 2)
            dve.tensor_tensor(fold[:, :], ident[:, 0:HD], ident[:, HD:P], ALU.add).then_inc(dconsts, 1)
            dve.wait_ge(g1_in, 16)
            for t in range(NT + 1):
                if t < NT:
                    scale(t, hn1, g1_row, 0)
                if t >= 1:
                    for c in range(2):
                        n = 2 * (t - 1) + c
                        dve.wait_ge(acc_hi, n + 1)
                        norm_lo(n % NACC, t - 1, c)
                if t in (HT, HT + 1):
                    split_mixer(mixer_ring(0), t - HT)
            dve.wait_ge(params_turned, 1)
            dve.tensor_copy(params[:, :], pv_out[:, 0:NCW + 5 * NJ]).then_inc(params_ready, 1)
            dve.wait_ge(params_ready, 1)
            dve.wait_ge(tables_in, 32)
            dve.wait_ge(consts, 9)

            def mixer(kind, j):
                steps = MIX[kind]
                ring = mixer_ring(j)
                accs, turns = numbered(steps, ACC_KINDS), numbered(steps, TURN_KINDS)
                acc0, turn0 = mixer_base(ACC_KINDS, j, NORM1_ACC), mixer_base(TURN_KINDS, j)
                his = numbered(steps, TURN_HI_KINDS)
                hi0 = mixer_base(TURN_HI_KINDS, j)
                scores = numbered(steps, ("qk",))
                lo, up = slice(0, HD), slice(HD, P)
                last_read = -1
                if kind == "loop":
                    dve.tensor_copy(now[:, 3:4], attn_g[:, bass.ds(j - 1, 1)])
                    dve.tensor_copy(now[:, 4:5], conv_g[:, bass.ds(j - 1, 1)])
                if kind == "last":
                    dve.tensor_copy(now[:, 3:4], attn_g[:, j - 1:j])
                    dve.tensor_copy(now[:, 4:5], conv_g[:, j - 1:j]).then_inc(now_ready, 1)
                else:
                    dve.tensor_copy(now[:, 0:3], mix_w[:, :, bass.ds(j, 1)].rearrange("p k a -> p (k a)"))\
                       .then_inc(now_ready, 1)
                dve.wait_ge(now_ready, j + 1)
                for s in steps:
                    if s[0] == "split":
                        if kind != "last":
                            split_mixer(ring, s[1])
                    elif s[0] == "proj" and s[3] == 3:
                        n = accs[s[:3]]
                        p, cols = acc[n % NACC], slice(s[2] * HALF, (s[2] + 1) * HALF)
                        if s[1] in "qk":
                            dve.wait_ge(acc_hi, j * 4 + (2 * NT + "qk".index(s[1]) * 2 + s[2] + 1))
                        else:
                            dve.wait_ge(acc_full, acc0 + (n + 1))
                        if s[1] == "q":
                            dve.scalar_tensor_tensor(out=Q[0][up, cols], in0=p[lo, :], scalar=HD ** -0.5,
                                                     in1=Q[0][lo, cols].bitcast(F32), op0=ALU.mult, op1=ALU.subtract)
                            dve.scalar_tensor_tensor(out=Q[1][lo, cols], in0=p[up, :], scalar=HD ** -0.5,
                                                     in1=Q[1][up, cols].bitcast(F32), op0=ALU.mult, op1=ALU.subtract)\
                               .then_inc(acc_drained, 1)
                        elif s[1] == "k":
                            dve.tensor_tensor(K1[0][up, cols], p[lo, :], K1[0][lo, cols].bitcast(F32), ALU.subtract)
                            dve.tensor_tensor(K2[0][lo, cols], p[lo, :], K1[0][lo, cols].bitcast(F32), ALU.subtract)
                            dve.tensor_tensor(K1[1][lo, cols], p[up, :], K1[1][up, cols].bitcast(F32), ALU.subtract)
                            dve.tensor_tensor(K2[1][up, cols], p[up, :], K1[1][up, cols].bitcast(F32), ALU.subtract)\
                               .then_inc(acc_drained, 1)
                        elif s[1] == "v":
                            dve.tensor_copy(prob[:, 1, cols], p[:, :]).then_inc(acc_drained, 1)
                        elif s[1] == "c":
                            dve.tensor_copy(cu[:, 2 + s[2] * HALF:2 + (s[2] + 1) * HALF], p[:, :]).then_inc(acc_drained, 1)
                        elif s[1] == "u":
                            part = cu[:, 2 + s[2] * HALF:2 + (s[2] + 1) * HALF]
                            dve.wait_ge(acc_drained, acc0 + (accs[("proj", "c", 1)] + 1))
                            dve.tensor_tensor(part, p[:, :], part, ALU.mult).then_inc(acc_drained, 1)
                        elif s[1] == "b":
                            if s[2] == 0:
                                dve.wait_ge(tap_ready, j + 1)
                                for tap in (1, 0):
                                    then_chain(dve.scalar_tensor_tensor(
                                        out=y[:, :], in0=cu[:, tap:tap + S], scalar=now[:, tap:tap + 1],
                                        in1=y[:, :], op0=ALU.mult, op1=ALU.add))
                            dve.tensor_tensor(y[:, cols], p[:, :], y[:, cols], ALU.mult).then_inc(acc_drained, 1)
                    elif s[0] == "vT":
                        dve.wait_ge(turn_hi, hi0 + (his[s] + 1))
                        src = turn[:, :].rearrange("p (t h d) -> p t h d", t=HT, h=2)
                        vs = V[:, HT * s[1]:HT * s[1] + HT, :, :]
                        dve.tensor_tensor(vs[:, :, :, HD:P], src, vs[:, :, :, 0:HD].bitcast(F32),
                                          ALU.subtract).then_inc(turn_drained, 1)
                        last_read = turns[s]
                    elif s[0] == "attT":
                        dve.wait_ge(turn_hi, hi0 + (his[s] + 1))
                        dve.scalar_tensor_tensor(out=half(mixA_lo, s[1]), in0=turn[:, :],
                                                 scalar=now[:, 3:4],
                                                 in1=half(mixA_hi, s[1]).bitcast(F32),
                                                 op0=ALU.mult, op1=ALU.subtract).then_inc(turn_drained, 1)
                    elif s[0] == "stat":
                        hf = s[1]
                        r = cu[:, 2 + hf * HALF:2 + (hf + 1) * HALF]
                        dve.wait_ge(y_r_ready, (j - 1) * 2 + (hf + 1))
                        dve.scalar_tensor_tensor(out=half(y, hf), in0=half(y, hf), scalar=now[:, 4:5],
                                                 in1=r, op0=ALU.mult, op1=ALU.mult).then_inc(turn_drained, 1)
                    elif s[0] == "yhi":
                        hf = s[1]
                        dve.wait_ge(y_hi, (j - 1) * 2 + (hf + 1))
                        dve.tensor_tensor(half(mixC_lo, hf), half(y, hf), half(mixC_hi, hf).bitcast(F32),
                                          ALU.subtract).then_inc(y_lo, 1)
                    elif s[0] == "out":
                        n = accs[s]
                        part = half(res[:, s[1] // 2, :], s[1] % 2)
                        dve.wait_ge(acc_full, acc0 + (n + 1))
                        dve.tensor_tensor(part, acc[n % NACC][:, :], part, ALU.add).then_inc(acc_drained, 1)
                    elif s[0] == "qk":
                        _, hd, qb = s
                        n, sl = P * (qb + 1), qb % 2
                        dve.wait_ge(score_full, j * (2 * NT) + (scores[s] + 1))
                        if last_read >= 0:
                            dve.wait_ge(turn_full, turn0 + (last_read + 1))
                        dve.memset(marker[:, 0:1], 0.0)
                        then_chain(dve.tensor_tensor_reduce(
                            prob[:, sl, 0:n], score[:, 0:n], bias[:, S - P - P * qb:S - P - P * qb + n], 1.0, -3e38,
                            ALU.add, ALU.max, m_raw[:, sl:sl + 1]))
                        dve.tensor_scalar(m_neg[:, sl:sl + 1], m_raw[:, sl:sl + 1], -1.0, None,
                                          ALU.mult).then_inc(logits_ready, 1)
                        if qb == NT - 1:
                            then_chain(dve.scalar_tensor_tensor(out=bias[:, :], in0=bias[:, :], scalar=0.5,
                                                                in1=half_log[:, :], op0=ALU.mult, op1=ALU.add))
                    elif s[0] == "tp":
                        _, hd, g, p = s
                        dve.wait_ge(turn_hi, hi0 + (his[s] + 1))
                        src = turn[:, :].rearrange("p (k q) -> p k q", k=2)
                        if p < g:
                            dve.tensor_tensor(probT_lo[:, reg_slot(s), :, :], src,
                                              probT_hi[:, reg_slot(s), :, :].bitcast(F32),
                                              ALU.subtract).then_inc(turn_drained, 1)
                        else:
                            dve.tensor_tensor(diagT_lo[:, 0, :], src[:, 0, :], diagT_hi[:, 0, :].bitcast(F32),
                                              ALU.subtract)
                            dve.tensor_tensor(diagT_lo[:, 1, P:256], src[:, 1, P:256],
                                              diagT_hi[:, 1, P:256].bitcast(F32), ALU.subtract).then_inc(turn_drained, 1)
                        last_read = turns[s]
                    elif s[0] == "otok":
                        hd = s[1]
                        n = turns[s]
                        dve.wait_ge(turn_full, turn0 + (n + 1))
                        then_chain(dve.reciprocal(l_inv[:, :], l_sum[:, hd, :]))
                        src = turn[:, :].rearrange("p (t d) -> p t d", t=NT)
                        dve.tensor_tensor(o_tok[:, :, :], src, l_inv[:, :].unsqueeze(2).to_broadcast([P, NT, HD]),
                                          ALU.mult).then_inc(turn_drained, 1)
                        dve.wait_ge(turn_drained, turn0 + (n + 1))
                        then_chain(dve.scalar_tensor_tensor(out=o_sq[:, :, :], in0=o_tok[:, :, :], scalar=1.0 / HD,
                                                            in1=o_tok[:, :, :], op0=ALU.mult, op1=ALU.mult))
                        dve.tensor_reduce(o_ss[:, :], o_sq[:, :, :], AX.X, ALU.add).then_inc(o_ss_ready, 1)
                    elif s[0] == "oscale":
                        hd = s[1]
                        dve.wait_ge(o_r_ready, j * 2 + (hd + 1))
                        dve.tensor_tensor(att[:, :, hd * HD:(hd + 1) * HD], o_tok[:, :, :],
                                          o_r[:, :].unsqueeze(2).to_broadcast([P, NT, HD]), ALU.mult).then_inc(att_ready, 1)
                    elif s[0] == "scale":
                        if s[1] == 0:
                            dve.wait_ge(g2_in, 16)
                        scale(s[1], hn2, g2_row, NT)
                    elif s[0] == "nT":
                        n = accs[s]
                        dve.wait_ge(acc_hi, 2 * NT + 4 * NJ + 2 * s[1] + s[2] + 1)
                        norm_lo(n % NACC, s[1], s[2])
                    if s == ("attT", 1) and kind == "last":
                        for k in range(3):
                            split_ffn(ffn_ring(0), k)

            mixer("first", 0)
            start = chain["n"]
            per = chained(MIX["loop"], NT)
            with dve.Fori(1, NJ) as j:
                chain.update(base=(j - 1) * per + start, n=0)
                mixer("loop", j)
                assert chain["n"] == per
            chain.update(base=start + (NJ - 1) * per, n=0)
            mixer("last", NJ)
            dve.memset(ub["g"][:, 0:2], 0.0)
            dve.memset(ub["v"][:, 0:2], 0.0).then_inc(pads, 1)
            dve.wait_ge(pads, 1)

            def ffn(kind, i):
                steps = FFN[kind]
                ring = ffn_ring(i)
                accs = numbered(steps, ACC_KINDS)
                acc0 = ffn_base(ACC_KINDS, i, MIX_ACC)
                ups = numbered(steps, ("up",))
                for s in steps:
                    if s[0] == "split":
                        split_ffn(ring, s[1])
                    elif s[0] == "up":
                        _, what, a, hf = s
                        zh = half(z[what], hf)
                        col = i * 2 + (a + (FTILES if what == "v" else 0))
                        dve.wait_ge(u_ready, i * 8 + (ups[s] + 1))
                        then_chain(dve.scalar_tensor_tensor(
                            out=zh, in0=ub[what][:, 1 + hf * HALF:1 + (hf + 1) * HALF],
                            scalar=ffn_w[:, 1, bass.ds(col, 1)], in1=zh, op0=ALU.mult, op1=ALU.add))
                        dve.scalar_tensor_tensor(
                            out=zh, in0=ub[what][:, hf * HALF:(hf + 1) * HALF],
                            scalar=ffn_w[:, 0, bass.ds(col, 1)], in1=zh, op0=ALU.mult, op1=ALU.add).then_inc(acc_drained, 1)
                    elif s[0] == "prod":
                        _, a, hf = s
                        n = i * 4 + (2 * a + hf + 1)
                        zg, zv = half(z["g"], hf), half(z["v"], hf)
                        dve.wait_ge(silu_done, n)
                        dve.wait_ge(acc_drained, acc0 + (accs[("up", "v", a, hf)] + 1))
                        dve.tensor_tensor(zg, zg, zv, ALU.mult).then_inc(prod_done, 1)
                        dve.wait_ge(a_hi_done, n)
                        dve.tensor_tensor(half(a_lo[:, a, :], hf), zg, half(a_hi[:, a, :], hf).bitcast(F32),
                                          ALU.subtract).then_inc(a_lo_done, 1)
                    elif s[0] == "down":
                        n = accs[s]
                        part = half(res[:, s[1] // 2, :], s[1] % 2)
                        dve.wait_ge(acc_full, acc0 + (n + 1))
                        dve.tensor_tensor(part, acc[n % NACC][:, :], part, ALU.add).then_inc(acc_drained, 1)
                    elif s[0] == "finish":
                        if s[1] == 0:
                            dve.wait_ge(gf_in, 16)
                        scale(s[1], hn2, gf_row, 2 * NT)

            start = start + (NJ - 1) * per + chain["n"]
            chain.update(base=start, n=0)
            ffn("first", 0)
            with dve.Fori(1, NI) as i:
                chain.update(base=i * 8 + start, n=0)
                ffn("loop", i)
                assert chain["n"] == 8
            chain.update(base=start + NI * 8, n=0)
            ffn("last", NI)

        @block.tensor
        def _(pe):
            def product(p, lhs, rhs, first, last):
                (l_hi, l_lo), (r_hi, r_lo) = lhs, rhs
                pe.matmul(p, l_hi, r_hi, start=first, stop=False)
                pe.matmul(p, l_hi, r_lo, start=False, stop=False)
                return pe.matmul(p, l_lo, r_hi, start=False, stop=last)

            def turn_norm(bank, hn, t, c):
                for k in range(4):
                    ins = pe.transpose(acc[bank][:, k * P:(k + 1) * P],
                                       hn[:, t % 2, (4 * c + k) * P:(4 * c + k + 1) * P], ident[:, :])
                ins.then_inc(acc_full, 1)

            def free_acc(n):
                pe.wait_ge(acc_drained, n - (NACC - 1))

            pe.wait_ge(consts, 6)
            for t in range(NT):
                pe.wait_ge(scaled, t + 1)
                for c in range(2):
                    if 2 * t + c >= NACC:
                        free_acc(2 * t + c)
                    turn_norm((2 * t + c) % NACC, hn1, t, c)
                if t == 1:
                    pe.wait_ge(rows_in, 64)
                    at = 0
                    for k in range(8):
                        rows = 2 * FTILES if k < 3 else NJ
                        ins = pe.transpose(pv_out[:, at:at + rows], param_rows[0:rows, k, :], ident[0:rows, 0:rows])
                        at += rows
                    ins.then_inc(params_turned, 1)
            pe.wait_ge(dconsts, 1)
            pe.wait_ge(params_ready, 1)

            def mixer(kind, j):
                steps = MIX[kind]
                tiles = mixer_tiles(kind)
                ring = mixer_ring(j)
                accs, turns = numbered(steps, ACC_KINDS), numbered(steps, TURN_KINDS)
                acc0, turn0 = mixer_base(ACC_KINDS, j, NORM1_ACC), mixer_base(TURN_KINDS, j)
                scores = numbered(steps, ("qk",))
                groups = 0

                def weights(tile):
                    sl = ring.slot(tiles.index(tile))
                    return whi[:, sl, :], wlo[:, sl, :]

                def free_turn(s):
                    if not (kind == "first" and turns[s] == 0):
                        pe.wait_ge(turn_drained, turn0 + turns[s])

                for s in steps:
                    if s[0] == "proj":
                        _, tile, hf, c = s
                        n = accs[s[:3]]
                        if c == 0:
                            free_acc(acc0 + n)
                            if kind == "first" and tile == "q":
                                pe.wait_ge(acc_drained, (hf + 1) * NT)
                            if hf == 0:
                                pe.wait_ge(w_made, ring.n(tiles.index(tile)) + 1)
                        w_hi, w_lo = weights(tile)
                        for k in (2 * c, 2 * c + 1):
                            ins = product(acc[n % NACC][:, :],
                                          (w_hi[:, k * P:(k + 1) * P], w_lo[:, k * P:(k + 1) * P]),
                                          (half(h_hi[:, k, :], hf), half(h_lo[:, k, :], hf)), k == 0, k == KT - 1)
                        if c == 3:
                            ins.then_inc(acc_full, 1)
                    elif s[0] == "vT":
                        hf = s[1]
                        free_turn(s)
                        pe.wait_ge(acc_drained, acc0 + (accs[("proj", "v", hf)] + 1))
                        for t in range(HT):
                            ins = pe.transpose(turn[:, t * P:(t + 1) * P],
                                               prob[:, 1, (HT * hf + t) * P:(HT * hf + t + 1) * P], ident[:, :])
                        ins.then_inc(turn_full, 1)
                    elif s[0] == "attT":
                        hf = s[1]
                        free_turn(s)
                        pe.wait_ge(att_ready, j * 2)
                        for t in range(HT):
                            ins = pe.transpose(turn[:, t * P:(t + 1) * P], att[:, HT * hf + t, :], ident[:, :])
                        ins.then_inc(turn_full, 1)
                    elif s[0] == "stat":
                        free_turn(s)
                        pe.wait_ge(y_squared, j)
                        pe.matmul(turn[:, :], mean64[:, :], cu[:, 2 + s[1] * HALF:2 + (s[1] + 1) * HALF],
                                  start=True, stop=True).then_inc(turn_full, 1)
                    elif s[0] == "out":
                        n = accs[s]
                        t, hf = s[1] // 2, s[1] % 2
                        free_acc(acc0 + n)
                        if s[1] == 0:
                            pe.wait_ge(w_made, ring.n(tiles.index("oC")) + 1)
                            pe.wait_ge(turn_drained, turn0 + (turns[("attT", 1)] + 1))
                            pe.wait_ge(y_lo, j * 2)
                        toks = slice(t * P, (t + 1) * P)
                        wa, wc = weights("oA"), weights("oC")
                        product(acc[n % NACC][:, :], (mixA_hi[:, toks], mixA_lo[:, toks]),
                                (half(wa[0], hf), half(wa[1], hf)), True, False)
                        product(acc[n % NACC][:, :], (mixC_hi[:, toks], mixC_lo[:, toks]),
                                (half(wc[0], hf), half(wc[1], hf)), False, True).then_inc(acc_full, 1)
                    elif s[0] == "qk":
                        _, hd, qb = s
                        if scores[s] == 0:
                            pe.wait_ge(acc_drained, acc0 + (accs[("proj", "k", 1)] + 1))
                        if not (kind == "first" and scores[s] == 0):
                            pe.wait_ge(logits_ready, j * (2 * NT) + scores[s])
                        q = Q[hd][:, qb * P:(qb + 1) * P]
                        for at, n in keys_of(qb):
                            pe.matmul(score[:, at:at + n], q, K1[hd][:, at:at + n], start=True, stop=False)
                            ins = pe.matmul(score[:, at:at + n], q, K2[hd][:, at:at + n], start=False, stop=True)
                        ins.then_inc(score_full, 1)
                    elif s[0] == "tp":
                        _, hd, g, p = s
                        free_turn(s)
                        if p == 0:
                            pe.wait_ge(probs_ready, j * (2 * NT) + (hd * NT + 2 * g + 2))
                        for kb in range(2):
                            for q in range(2):
                                if p == g and kb == 1 and q == 0:
                                    continue
                                k = 2 * p + kb
                                ins = pe.transpose(turn[:, kb * 256 + q * P:kb * 256 + (q + 1) * P],
                                                   prob[:, q, k * P:(k + 1) * P], ident[:, :])
                        ins.then_inc(turn_full, 1)
                    elif s[0] == "pv":
                        _, hd, g, p = s
                        pe.wait_ge(turn_drained, turn0 + (turns[("tp", hd, g, p)] + 1))
                        if p == 0 and not (kind == "first" and groups == 0):
                            pe.wait_ge(o_copied, j * NT + groups)
                        for kb in range(2):
                            k = 2 * p + kb
                            v = V[:, k, hd, :]
                            for n, part in enumerate((probT_hi, probT_lo) if p < g else (diagT_hi, diagT_lo)):
                                src = part[:, reg_slot(s), kb, :] if p < g else part[:, kb, :]
                                ins = pe.matmul(pv_out[:, 0:256], v, src, start=(k == 0 and n == 0),
                                                stop=(k == 2 * g + 1 and n == 1))
                        ins.then_inc(pv_done, 1)
                        if p == g:
                            groups += 1
                    elif s[0] == "otok":
                        hd = s[1]
                        free_turn(s)
                        pe.wait_ge(o_copied, j * NT + (hd + 1) * (NT // 2))
                        for t in range(NT):
                            ins = pe.matmul(turn[:, t * HD:(t + 1) * HD], o_sb[:, t * P:(t + 1) * P], fold[:, :],
                                            start=True, stop=True)
                        ins.then_inc(turn_full, 1)
                    elif s[0] == "nT":
                        n = accs[s]
                        free_acc(acc0 + n)
                        pe.wait_ge(scaled, NT + s[1] + 1)
                        turn_norm(n % NACC, hn2, s[1], s[2])

            mixer("first", 0)
            with pe.Fori(1, NJ) as j:
                mixer("loop", j)
            mixer("last", NJ)

            def ffn(kind, i):
                steps = FFN[kind]
                tiles = ffn_tiles(kind)
                ring = ffn_ring(i)
                accs = numbered(steps, ACC_KINDS)
                acc0 = ffn_base(ACC_KINDS, i, MIX_ACC)

                def weights(tile):
                    sl = ring.slot(tiles.index(tile))
                    return fhi[:, sl, :], flo[:, sl, :]

                for s in steps:
                    if s[0] == "up":
                        _, what, a, hf = s
                        n = accs[s]
                        tile = f"{what}{a}"
                        free_acc(acc0 + n)
                        if kind == "first" and tile == "g0":
                            done = mixer_base(ACC_KINDS, NJ, NORM1_ACC)
                            done += numbered(MIX["last"], ACC_KINDS)[("nT", HT * (hf + 1) - 1, 1)] + 1
                            pe.wait_ge(acc_drained, done)
                        if hf == 0:
                            pe.wait_ge(f_made, ring.n(tiles.index(tile)) + 1)
                        w_hi, w_lo = weights(tile)
                        for k in range(KT):
                            ins = product(acc[n % NACC][:, :],
                                          (w_hi[:, k * P:(k + 1) * P], w_lo[:, k * P:(k + 1) * P]),
                                          (half(h_hi[:, k, :], hf), half(h_lo[:, k, :], hf)), k == 0, k == KT - 1)
                        ins.then_inc(acc_full, 1)
                    elif s[0] == "down":
                        n = accs[s]
                        t, hf = s[1] // 2, s[1] % 2
                        free_acc(acc0 + n)
                        if s[1] == 0:
                            pe.wait_ge(f_made, ring.n(tiles.index("dB")) + 1)
                            pe.wait_ge(a_lo_done, i * 4)
                        toks = slice(t * P, (t + 1) * P)
                        for a, tile in enumerate(("dA", "dB")):
                            w = weights(tile)
                            ins = product(acc[n % NACC][:, :], (a_hi[:, a, toks], a_lo[:, a, toks]),
                                          (half(w[0], hf), half(w[1], hf)), a == 0, a == 1)
                        ins.then_inc(acc_full, 1)

            ffn("first", 0)
            with pe.Fori(1, NI) as i:
                ffn("loop", i)
            ffn("last", NI)


def bias_tables(S):
    import numpy as np
    dist = (S - P + np.arange(P)[:, None] - np.arange(S)[None, :]).astype(np.int64)
    seen = sum(((dist >= 0) & (dist <= window) & (dist % dilation == 0)).astype(np.int64)
               for window, dilation in ((128, 1), (512, 4), (2048, 16)))
    logs = np.where(seen > 0, np.log(np.maximum(seen, 1)), MASKED)
    first = np.where(seen > 0, -0.5 * dist + logs, MASKED)
    return first.astype(np.float32), (0.5 * logs).astype(np.float32)


_INS = ["x", "norm1_g", "w_in", "mix_conv_w", "attn_out_g", "conv_out_g", "w_out", "norm2_g", "ffn_up",
        "ffn_conv_w", "ffn_down", "final_norm_g"]


def kernel(**inputs):
    import numpy as np
    import concourse.bacc as bacc
    from concourse.bass_utils import run_bass_kernel_spmd

    nc = bacc.Bacc("TRN2", target_bir_lowering=False, num_devices=1, dynamic_dma_scratch_size=1024)
    arrays = {f"in_{n}": np.ascontiguousarray(inputs[n]) for n in _INS}
    arrays["in_bias"], arrays["in_logs"] = bias_tables(inputs["x"].shape[1])
    args = [nc.dram_tensor(n, a.shape, mybir.dt.from_np(a.dtype), kind="ExternalInput").ap() for n, a in arrays.items()]
    out = nc.dram_tensor("out", inputs["x"].shape, F32, kind="ExternalOutput").ap()
    build_program(nc, *args, out)
    r = run_bass_kernel_spmd(nc, [arrays], core_ids=[0])
    return r.results[0]["out"]
```

```python
from contextlib import ExitStack

import concourse.bass as bass
from concourse import mybir

F32 = mybir.dt.float32
F32R = mybir.dt.float32r
ALU = mybir.AluOpType
ACT = mybir.ActivationFunctionType
AX = mybir.AxisListType

P = 128
EPS = 1e-6
MASKED = -1e30


class Ring:

    def __init__(self, depth, turns, rest):
        self.depth, self.turns, self.rest = depth, turns, rest

    def n(self, k):
        return self.turns * self.depth + (self.rest + k)

    def slot(self, k):
        return (self.rest + k) % self.depth

    def turn(self, k):
        return self.turns + (self.rest + k) // self.depth


def mixer_tiles(kind):
    if kind == "first":
        return ["q", "k", "v", "c", "u", "b"]
    if kind == "last":
        return ["oC", "oA"]
    return ["q", "k", "v", "c", "u", "b", "oA", "oC"]


SLOTS = {"first": [2, 0, 1, 0, 1, 2, 2], "loop": [2, 0, 1, 0, 1, 2, 0, 1, 2], "last": [2, 0]}


def ffn_tiles(kind):
    if kind == "first":
        return ["g0", "v0", "g1", "v1"]
    if kind == "last":
        return ["dA", "dB"]
    return ["g0", "dA", "dB", "v0", "g1", "v1"]


def proj(tile, half):
    return [("proj", tile, half, c) for c in range(4)]


def up(what, a, half):
    return [("up", what, a, half, c) for c in range(4)]


ORDER = {
    "first": ["Vv3vvqleqvl.eV", ".qltq.plece", "ql.t.qlt.eepp", "cqltteqp.lte", "q.ptpqtcll.tptep.eppc",
              "qo.l..tq.plec.e", "sqltt.qlp.pe....ce", "qtl.tt....q.....lp.peepc", "t..t.pt..tp.p.",
              "..pcOS...."],
    "loop": ["vvvvv3qlvveqvlVe..V.", "t.qq.pll.ece", "qlt.tq.el.e.", "qltpptqlce..t.epppc",
             "qqlett.pt.pletp..", "pqct.loql.pce.e.", ".tqtl..se.q.l.ep..p", "tqlct..pt.q.ep.lp...ec",
             "tt..ptt..p.", ".................ppc...OS"],
}


def first_norm_steps(NT):
    def ahead(t):
        return [("square", t), ("scale", t)] if t < NT else []

    steps = ahead(0) + ahead(1)
    for t in range(NT // 2):
        steps += [("nT", t, 0), ("nT", t, 1)] + ahead(t + 2)
        if t >= 2:
            steps.append(("split", t - 2))
    steps.append(("split", 2))
    side = proj("q", 0) + proj("k", 0) + proj("v", 0)
    for t in range(NT // 2, NT):
        steps += side[:3] + [("nT", t, 0), ("nT", t, 1)] + ahead(t + 2)
        side = side[3:]
    return steps + [("params",)] + proj("q", 1) + proj("k", 1)


def mixer_steps(kind, NT):
    if kind == "first":
        steps = first_norm_steps(NT)
    else:
        tail = {1: [("yhi", 0), ("yhi", 1)], 3: [("split", 1)], 4: [("attT", 0)], 5: [("attT", 1)], 7: [("split", 2)]}
        steps = []
        for n, c in enumerate(proj("q", 0) + proj("q", 1) + proj("k", 0) + proj("k", 1)):
            steps += [c] + tail.get(n, [])
    fill = [[c] for x in "cub" for c in proj(x, 0) + proj(x, 1)]
    fill[3].append(("split", 4))
    fill[5].append(("split", 5))
    if kind != "first":
        fill[12].append(("split", 6))
        fill[20].append(("split", 7))
        fill += [[("outC", b), ("out", b)] for b in range(2 * NT)]
        fill[26].append(("stat", 0))
        fill[27].append(("stat", 1))
        fill[28].append(("split", 8))

    groups = [(hd, g) for hd in range(2) for g in range(NT // 2)]
    queues = {
        "v": [[c] for c in (proj("v", 0) if kind != "first" else []) + proj("v", 1)],
        "V": [[("vT", 0)], [("vT", 1)]],
        "3": [[("split", 3)]],
        "t": [[("tp", hd, g, p)] for hd, g in groups for p in range(g + 1)],
        "p": [[("pv", hd, g, p)] for hd, g in groups for p in range(g + 1)],
        "c": [[("ocopy", hd, g)] for hd, g in groups],
        "o": [[("otok", 0, 0), ("otok", 0, 1), ("oroot", 0)]],
        "s": [[("oscale", 0)]],
        "O": [[("otok", 1, 0), ("otok", 1, 1), ("oroot", 1)]],
        "S": [[("oscale", 1)]],
        ".": fill,
    }
    for token, what in (("q", "qk"), ("l", "logits"), ("e", "exp")):
        queues[token] = [[(what, hd, qb)] for hd in range(2) for qb in range(NT)]
    for n, order in enumerate(ORDER[kind]):
        for token in order:
            if token != "." or fill:
                steps += queues[token].pop(0)
        done = 2 * min(n + 1, len(groups))
        assert all(len(queues[token]) == 2 * len(groups) - done for token in "qle")
        assert len(queues["t"]) == sum(g + 1 for hd, g in groups[n:])
    assert not any(queue for token, queue in queues.items() if token != ".")
    for f in fill:
        steps += f
    if kind == "first":
        steps += [("stat", 0), ("stat", 1), ("split", 6)]
    return steps


def bridge_steps(NT):
    at = {t: i for i, t in enumerate(ffn_tiles("first"))}
    steps = [("split", 1), ("yhi", 0), ("yhi", 1)]
    steps += [("outC", b) for b in range(4)] + [("attT", 0), ("attT", 1), ("pads",)]
    steps += [("fsplit", k) for k in range(3)]
    side = up("g", 0, 0) + up("v", 0, 0) + up("g", 1, 0)[:3]

    def beside(n=1):
        for _ in range(n):
            if side:
                steps.append(side.pop(0))

    for t in range(NT):
        for b in (2 * t, 2 * t + 1):
            steps += ([("outC", b)] if b >= 4 else []) + [("out", b)]
            if t >= 6:
                beside()
        steps.append(("square", t))
        if t >= 1:
            steps.append(("scale", t - 1))
        if t >= 2:
            steps += [("nT", t - 2, 0), ("nT", t - 2, 1)]
        if t >= 6:
            beside()
    steps.append(("scale", NT - 1))
    beside(2)
    steps += [("nT", NT - 2, 0), ("nT", NT - 2, 1)]
    beside(3)
    steps += [("nT", NT - 1, 0), ("nT", NT - 1, 1)]
    steps += [("silu", 0, 0)] + up("g", 0, 1) + [("fsplit", at["g0"] + 3), ("prod", 0, 0), ("silu", 0, 1)]
    steps += up("v", 0, 1) + [("prod", 0, 1)]
    steps += up("g", 1, 0)[3:] + up("g", 1, 1) + [("fsplit", at["v0"] + 3), ("fsplit", at["g1"] + 3)]
    steps += [("silu", 1, 0), ("silu", 1, 1)]
    steps += up("v", 1, 0) + [("prod", 1, 0)] + up("v", 1, 1) + [("prod", 1, 1)]
    return steps


def ffn_steps(kind, NT):
    tiles = ffn_tiles(kind)
    at = {t: i for i, t in enumerate(tiles)}
    blocks = range(2 * NT)
    if kind == "last":
        early = 5
        steps = [("downA", b) for b in range(early)]
        for b in blocks:
            steps += ([("downA", b)] if b >= early else []) + [("down", b)]
            t = b // 2
            if b % 2 == 1:
                steps.append(("fsquare", t))
            elif t >= 1:
                steps.append(("finish", t - 1))
        return steps + [("finish", NT - 1)]
    downs = [s for b in blocks for s in (("downA", b), ("down", b))]
    steps = [("fsplit", 2)]
    for a in range(2):
        steps += up("g", a, 0) + up("g", a, 1) + [("fsplit", at[f"g{a}"] + 3)]
        if a == 0:
            steps += downs + [("fsplit", at["dA"] + 3), ("fsplit", at["dB"] + 3)]
        steps += [("silu", a, 0), ("silu", a, 1)]
        steps += up("v", a, 0) + [("prod", a, 0)] + up("v", a, 1) + [("prod", a, 1)]
        if a == 0:
            steps.append(("fsplit", at["v0"] + 3))
    return steps


CHUNKED = ("proj", "up")


def key(s):
    return s[:-1] if s[0] in CHUNKED else s


def opens(s):
    if s[0] in CHUNKED:
        return key(s) if s[-1] == 0 else None
    return {"outC": ("out",) + s[1:], "downA": ("down",) + s[1:], "nT": s}.get(s[0])


def numbered(steps, kinds):
    out = {}
    for s in steps:
        if s[0] in kinds and not (s[0] in CHUNKED and s[-1] != 3):
            out[key(s)] = len(out)
    return out


def plan_banks(steps, entry, tail):
    number = numbered(steps, ACC_KINDS)
    last, busy, plan = dict(entry), {}, {}
    for s in steps:
        use = opens(s)
        if use:
            free = [b for b in last if b not in busy]
            bank = min(free, key=lambda b: (-99 if last[b] is None else last[b], b))
            left = len(number) - len(plan)
            if left <= len(tail) and tail[-left] in free:
                bank = tail[-left]
            plan[use] = (bank, last[bank])
            busy[bank] = use
        if key(s) in number and not (s[0] in CHUNKED and s[-1] != 3):
            bank = plan[key(s)][0]
            last[bank] = number[key(s)]
            del busy[bank]
    assert not busy
    return plan, {b: n - len(number) for b, n in last.items()}


def no_later(left, entry):
    return all(left[b] <= entry[b] for b in entry)


def reg_slot(s):
    _, hd, g, p = s
    return (hd * 6 + g * (g - 1) // 2 + p) % 2


def last_user(s, pvs):
    _, hd, g, p = s
    if p == g:
        return None
    order = [q for q in pvs if q[3] < q[2]]
    at = order.index(("pv", hd, g, p))
    return pvs[order[at - 2]] if at >= 2 else None


def chained(steps, NT):
    n = sum(s[0] == "logits" for s in steps)
    n += sum(1 + 4 * s[2] for s in steps if s[0] == "otok")
    n += sum(s[0] == "logits" and s[2] == NT - 1 for s in steps)
    return n + 2 * sum(s[:3] == ("proj", "b", 0) and s[3] == 3 for s in steps)


ACC_KINDS = ("proj", "out", "nT", "up", "down")
TURN_KINDS = ("vT", "tp", "otok", "attT", "stat")
TURN_HI_KINDS = ("vT", "tp", "attT")
MLP_STEPS = ("up", "fsplit", "silu", "prod", "downA", "down", "fsquare", "finish", "pads")


def build_program(nc, x, norm1_g, w_in, mix_conv_w, attn_out_g, conv_out_g, w_out, norm2_g, ffn_up,
                  ffn_conv_w, ffn_down, final_norm_g, bias_table, log_counts, out):
    _, S, D = x.shape
    NT = S // P
    KT = D // P
    HALF = S // 2
    HT = NT // 2
    HD = 64
    D_ATTN = attn_out_g.shape[1]
    NJ = D_ATTN // P
    F = ffn_down.shape[1]
    FTILES = F // P
    NI = FTILES // 2
    assert D == 2 * D_ATTN and S == 1024 and FTILES % 2 == 0 and KT == 8

    bridge = bridge_steps(NT)
    MIX = {"first": mixer_steps("first", NT), "loop": mixer_steps("loop", NT), "last": bridge}
    FFN = {"first": bridge, "loop": ffn_steps("loop", NT), "last": ffn_steps("last", NT)}

    def total(steps, kinds):
        return len(numbered(steps, kinds))

    def mixer_base(kinds, j, before=0):
        if isinstance(j, int) and j == 0:
            return before
        first, loop = total(MIX["first"], kinds), total(MIX["loop"], kinds)
        return j * loop + (before + first - loop)

    def ffn_base(kinds, i, before=0):
        if isinstance(i, int) and i == 0:
            return before
        first, loop = total(bridge, kinds), total(FFN["loop"], kinds)
        return i * loop + (before + first - loop)

    def hi_number(kind, j, s):
        def has_hi(t):
            return t[0] == "nT" or (t[0] == "proj" and t[1] in "qk" and t[3] == 3)
        before = sum(map(has_hi, MIX["first"])) - sum(map(has_hi, MIX["loop"]))
        base = 0 if kind == "first" else j * sum(map(has_hi, MIX["loop"])) + before
        own = [key(t) for t in MIX[kind] if has_hi(t)]
        return base + (own.index(key(s)) + 1)

    MIX_ACC = mixer_base(ACC_KINDS, NJ)
    MIX_ENTRY = {0: -4, 1: -1, 2: -2}
    FFN_ENTRY = {0: -4, 1: -4, 2: -4, 3: -3, 4: -2, 5: -1}
    MIX_TAIL, FFN_TAIL = [0, 1, 2, 1], list(range(6))
    PLAN = {}
    PLAN["m_first"], left = plan_banks(MIX["first"], {b: None for b in range(3)}, MIX_TAIL)
    assert no_later(left, MIX_ENTRY), left
    PLAN["m_loop"], left = plan_banks(MIX["loop"], MIX_ENTRY, MIX_TAIL)
    assert no_later(left, MIX_ENTRY), left
    PLAN["bridge"], left = plan_banks(bridge, {**MIX_ENTRY, 3: None, 4: None, 5: None}, FFN_TAIL)
    assert no_later(left, FFN_ENTRY), left
    PLAN["f_loop"], left = plan_banks(FFN["loop"], FFN_ENTRY, FFN_TAIL)
    assert no_later(left, FFN_ENTRY), left
    PLAN["f_last"], _ = plan_banks(FFN["last"], FFN_ENTRY, [])
    PLAN["m_last"] = PLAN["f_first"] = PLAN["bridge"]
    assert all(total(MIX[k], TURN_KINDS) % 2 == 0 for k in MIX)

    def tile_number(j, k):
        return k + 1 if isinstance(j, int) and j == 0 else j * 8 + (k - 1)

    def slot_loads(kind, j, k):
        slot = SLOTS[kind][k]
        first, loop = SLOTS["first"][:-1].count(slot), SLOTS["loop"][:-1].count(slot)
        own = SLOTS[kind][:k + 1].count(slot)
        return own if kind == "first" else j * loop + (first - loop + own)

    def ffn_ring(i):
        return Ring(3, 0, 0) if isinstance(i, int) and i == 0 else Ring(3, i * 2 - 1, 1)

    ctx = ExitStack()
    with ctx:
        def sb(name, shape, dt=F32, scope=ctx):
            return scope.enter_context(nc.sbuf_tensor(name, shape, dt))

        def sem(name):
            return ctx.enter_context(nc.semaphore(name))

        h_hi = sb("h_hi", [P, KT, S], F32R)
        h_lo = sb("h_lo", [P, KT, S], F32R)
        res = sb("res", [P, NT, D])
        ident = sb("ident", [P, P])
        mean64 = sb("mean64", [P, P])
        params = sb("params", [P, 3 * 2 * FTILES + 5 * NJ])
        ss = sb("ss", [P, NT])
        rstd = sb("rstd", [P, NT])
        eps = sb("eps", [P, 1])
        now = sb("now", [P, 5])
        NCW = 3 * 2 * FTILES
        ffn_w = params[:, 0:NCW].rearrange("p (k t) -> p k t", k=3)
        mix_w = params[:, NCW:NCW + 3 * NJ].rearrange("p (k t) -> p k t", k=3)
        attn_g = params[:, NCW + 3 * NJ:NCW + 4 * NJ]
        conv_g = params[:, NCW + 4 * NJ:NCW + 5 * NJ]

        with ExitStack() as scope:
            hn1 = sb("hn1", [P, 2, D], F32, scope)
            g1_row = sb("g1_row", [P, D], F32, scope)
            param_rows = sb("param_rows", [P, 8, P], F32, scope)
        with ExitStack() as scope:
            mixA_hi = sb("mixA_hi", [P, S], F32R, scope)
            mixA_lo = sb("mixA_lo", [P, S], F32R, scope)
            mixC_hi = sb("mixC_hi", [P, S], F32R, scope)
            mixC_lo = sb("mixC_lo", [P, S], F32R, scope)
            Q = [sb(f"Q{n}", [P, S], F32R, scope) for n in range(2)]
            K1 = [sb(f"K1_{n}", [P, S], F32R, scope) for n in range(2)]
            K2 = [sb(f"K2_{n}", [P, S], F32R, scope) for n in range(2)]
            V = sb("V", [P, NT, 2, P], F32R, scope)
            probT_hi = sb("probT_hi", [P, 2, 2, 256], F32R, scope)
            probT_lo = sb("probT_lo", [P, 2, 2, 256], F32R, scope)
            diagT_hi = sb("diagT_hi", [P, 2, 256], F32R, scope)
            diagT_lo = sb("diagT_lo", [P, 2, 256], F32R, scope)
            prob = sb("prob", [P, 4, S], F32, scope)
            bias = sb("bias", [P, S], F32, scope)
            half_log = sb("half_log", [P, S], F32, scope)
            o_sb = sb("o_sb", [P, S], F32, scope)
            m_raw = sb("m_raw", [P, 4], F32, scope)
            marker = sb("marker", [P, 1], F32, scope)
            m_neg = sb("m_neg", [P, 4], F32, scope)
            l_sum = sb("l_sum", [P, 2, NT], F32, scope)
            l_inv = sb("l_inv", [P, NT], F32, scope)
            o_ss = sb("o_ss", [P, NT], F32, scope)
            o_r = sb("o_r", [P, NT], F32, scope)
            att = sb("att", [P, NT, P], F32, scope)
            whi = sb("whi", [P, 3, 1024], F32R, scope)
            with ExitStack() as raw:
                wraw = sb("wraw", [P, 3, 1024], F32, raw)
            wlo = sb("wlo", [P, 3, 1024], F32R, scope)
            cu = sb("cu", [P, 2 + S], F32, scope)
            y = sb("y", [P, S], F32, scope)
        with ExitStack() as scope:
            gf_row = sb("gf_row", [P, D], F32, scope)
            sb("below_output_parts", [P, 3 * S], F32, scope)
            fraw = sb("fraw", [P, 3, 1024], F32, scope)
            g2_row = sb("g2_row", [P, D], F32, scope)
            hn2 = sb("hn2", [P, 2, D], F32, scope)
            fhi = sb("fhi", [P, 3, 1024], F32R, scope)
            flo = sb("flo", [P, 3, 1024], F32R, scope)
            ub = {n: sb(f"ub_{n}", [P, 2 + S], F32, scope) for n in "gv"}
            z = {n: sb(f"z_{n}", [P, S], F32, scope) for n in "gv"}
            a_hi = sb("a_hi", [P, 2, S], F32R, scope)
            a_lo = sb("a_lo", [P, 2, S], F32R, scope)

        turn = [ctx.enter_context(nc.psum_tensor(f"turn{n}", [P, 512], F32)) for n in range(2)]
        acc_banks = [ctx.enter_context(nc.psum_tensor(f"acc{n}", [P, 512], F32)) for n in range(3)]
        score = ctx.enter_context(nc.psum_tensor("score", [P, 1024], F32))
        pv_out = ctx.enter_context(nc.psum_tensor("pv_out", [P, 512], F32))
        banks = [t[:, :] for t in acc_banks] + [score[:, 0:512], score[:, 512:1024], pv_out[:, :]]

        def turn_of(turns, s):
            return turn[turns[s] % 2][:, :]

        class Accs:

            def __init__(self, phase, kind, n):
                steps = (MIX if phase == "m" else FFN)[kind]
                self.plan = PLAN[f"{phase}_{kind}"]
                self.own = numbered(steps, ACC_KINDS)
                self.base = mixer_base(ACC_KINDS, n) if phase == "m" else ffn_base(ACC_KINDS, n, MIX_ACC)

            def of(self, s):
                return banks[self.plan[key(s)][0]]

            def number(self, s):
                return self.base + (self.own[key(s)] + 1)

            def before(self, s):
                last = self.plan[key(s)][1]
                return None if last is None else self.base + (last + 1)

        x_in = [sem(f"x_in{t}") for t in range(NT)]
        tables_in = sem("tables_in")
        rows_in = sem("rows_in")
        g1_in, g2_in, gf_in = sem("g1_in"), sem("g2_in"), sem("gf_in")
        w_in_slot = [sem(f"w_in_slot{n}") for n in range(3)]
        f_in_slot = [sem(f"f_in_slot{n}") for n in range(3)]
        consts = sem("consts")
        params_turned = sem("params_turned")
        params_ready = sem("params_ready")
        w_hi_made, w_made = sem("w_hi_made"), sem("w_made")
        f_hi_made, f_made = sem("f_hi_made"), sem("f_made")
        squared = sem("squared")
        squared_log = sem("squared_log")
        rstd_ready = sem("rstd_ready")
        o_log, o_r_ready = sem("o_log"), sem("o_r_ready")
        y_log, y_r_ready = sem("y_log"), sem("y_r_ready")
        scaled = sem("scaled")
        acc_full, acc_drained = sem("acc_full"), sem("acc_drained")
        acc_hi = sem("acc_hi")
        turn_full, turn_drained, turn_hi = sem("turn_full"), sem("turn_drained"), sem("turn_hi")
        score_full = sem("score_full")
        logits_ready = sem("logits_ready")
        probs_ready = sem("probs_ready")
        pv_done = sem("pv_done")
        o_copied = sem("o_copied")
        att_ready = sem("att_ready")
        tap_ready = sem("tap_ready")
        now_ready = sem("now_ready")
        y_squared, y_hi, y_lo = sem("y_squared"), sem("y_hi"), sem("y_lo")
        pads = sem("pads")
        u_ready = sem("u_ready")
        silu_done, prod_done, a_hi_done, a_lo_done = sem("silu_done"), sem("prod_done"), sem("a_hi_done"), sem("a_lo_done")
        dve_chain = sem("dve_chain")
        stored = [sem(f"stored{n}") for n in range(2)]

        x_d = x[0].rearrange("(t p) d -> t p d", p=P)
        out_d = out[0].rearrange("(t p) d -> t p d", p=P)
        w_in_d = w_in[0].rearrange("(k p) c -> p k c", p=P)
        up_d = ffn_up[0].rearrange("(k p) c -> p k c", p=P)
        IN_AT = {"q": 0, "k": D_ATTN, "v": 2 * D_ATTN, "b": 3 * D_ATTN, "c": 3 * D_ATTN + D_ATTN, "u": 5 * D_ATTN}

        def half(t, n):
            return t[:, n * HALF:(n + 1) * HALF]

        def keys_of(qb):
            n = P * (qb + 1)
            pieces = [(0, min(max(n, 256), 512))]
            if n > 512:
                pieces.append((512, max(n - 512, 256)))
            return pieces

        def score_at(qb):
            return 512 if qb in (1, 3) else 0

        block = ctx.enter_context(nc.Block())

        @block.sync
        def _(sp):
            def mixer_weights(kind, j, ks):
                tiles, slots = mixer_tiles(kind), SLOTS[kind]
                accs = Accs("m", kind, j)
                for k in ks:
                    tile, slot = tiles[k], slots[k]
                    earlier = [n for n in range(k) if slots[n] == slot]
                    if earlier:
                        before = tiles[earlier[-1]]
                        sp.wait_ge(acc_full, accs.number(("proj", before, 1, 3)))
                    elif kind != "first" and k == 0:
                        sp.wait_ge(y_squared, j)
                    elif kind != "first":
                        sp.wait_ge(acc_full, accs.base)
                    dst = wraw[:, slot, :]
                    if tile[0] == "o":
                        row = (j - 1) * P + (0 if tile == "oA" else D_ATTN)
                        src = w_out[0][bass.ds(row, P), :]
                    else:
                        src = w_in_d[:, :, bass.ds(j * P + IN_AT[tile], P)]
                        dst = dst.rearrange("p (k c) -> p k c", k=KT)
                    sp.dma_start(dst, src).then_inc(w_in_slot[slot], 16)

            def ffn_weights(kind, i):
                ring = ffn_ring(i)
                for k, tile in enumerate(ffn_tiles(kind)):
                    if not (kind == "first" and k < 3):
                        sp.wait_ge(f_made, ring.n(k) - 2)
                    dst = fraw[:, ring.slot(k), :]
                    if tile[0] == "d":
                        row = (i - 1) * (2 * P) + (0 if tile == "dA" else P)
                        src = ffn_down[0][bass.ds(row, P), :]
                    else:
                        col = i * (2 * P) + (int(tile[1]) * P + (F if tile[0] == "v" else 0))
                        src = up_d[:, :, bass.ds(col, P)]
                        dst = dst.rearrange("p (k c) -> p k c", k=KT)
                    sp.dma_start(dst, src).then_inc(f_in_slot[ring.slot(k)], 16)

            sp.dma_start(res[:, 0, :], x_d[0]).then_inc(x_in[0], 16)
            sp.dma_start(g1_row[:], norm1_g[0].partition_broadcast(P)).then_inc(g1_in, 16)
            for t in range(1, HT):
                sp.dma_start(res[:, t, :], x_d[t]).then_inc(x_in[t], 16)
            mixer_weights("first", 0, range(3))
            for t in range(HT, NT):
                sp.dma_start(res[:, t, :], x_d[t]).then_inc(x_in[t], 16)
            sp.dma_start(param_rows[0:2 * FTILES, 0:3, :],
                         ffn_conv_w[0].rearrange("k (t p) -> t k p", p=P)).then_inc(rows_in, 16)
            sp.dma_start(param_rows[0:NJ, 3:6, :],
                         mix_conv_w[0].rearrange("k (t p) -> t k p", p=P)).then_inc(rows_in, 16)
            sp.dma_start(param_rows[0:NJ, 6, :], attn_out_g[0].rearrange("(t p) -> t p", p=P)).then_inc(rows_in, 16)
            sp.dma_start(param_rows[0:NJ, 7, :], conv_out_g[0].rearrange("(t p) -> t p", p=P)).then_inc(rows_in, 16)
            sp.dma_start(bias[:], bias_table).then_inc(tables_in, 16)
            sp.dma_start(half_log[:], log_counts).then_inc(tables_in, 16)
            mixer_weights("first", 0, range(3, 6))
            with sp.Fori(1, NJ) as j:
                mixer_weights("loop", j, range(8))
            mixer_weights("last", NJ, range(2))
            sp.wait_ge(score_full, 2 * NT * NJ)
            sp.dma_start(g2_row[:], norm2_g[0].partition_broadcast(P)).then_inc(g2_in, 16)
            ffn_weights("first", 0)
            mixed = Accs("m", "last", NJ)
            sp.wait_ge(acc_full, mixed.number(("out", 2 * NT - 1)))
            sp.dma_start(gf_row[:], final_norm_g.partition_broadcast(P)).then_inc(gf_in, 16)
            with sp.Fori(1, NI) as i:
                ffn_weights("loop", i)
            ffn_weights("last", NI)
            for t in range(NT):
                sp.wait_ge(scaled, 2 * NT + t + 1)
                sp.dma_start(out_d[t], hn2[:, t % 2, :]).then_inc(stored[t % 2], 16)
            for s in stored:
                sp.wait_ge(s, 16 * (NT // 2))

        @block.gpsimd
        def _(pool):
            pool.memset(ident[:], 0.0).then_inc(consts, 1)
            pool.wait_ge(consts, 1)
            pool.affine_select(out=ident[:], in_=ident[:], compare_op=ALU.not_equal, fill=1.0, base=0,
                               pattern=[[-1, P]], channel_multiplier=1).then_inc(consts, 1)
            pool.wait_ge(consts, 2)
            pool.memset(eps[:], EPS).then_inc(consts, 1)
            pool.wait_ge(consts, 3)
            pool.memset(mean64[:], 0.0).then_inc(consts, 1)
            pool.wait_ge(consts, 4)
            pool.memset(mean64[0:HD, 0:HD], 1.0 / HD).then_inc(consts, 1)
            pool.wait_ge(consts, 5)
            pool.memset(mean64[HD:P, HD:P], 1.0 / HD).then_inc(consts, 1)
            pool.wait_ge(consts, 6)
            pool.memset(cu[:, 0:2], 0.0).then_inc(consts, 1)
            pool.wait_ge(consts, 7)
            pool.memset(diagT_hi[:, 1, 0:P].bitcast(F32), 0.0).then_inc(consts, 1)
            pool.wait_ge(consts, 8)
            pool.memset(diagT_lo[:, 1, 0:P].bitcast(F32), 0.0).then_inc(consts, 1)

        @block.scalar
        def _(act):
            def split_mixer(kind, j, k):
                slot = SLOTS[kind][k]
                act.wait_ge(w_in_slot[slot], slot_loads(kind, j, k) * 16)
                act.activation(whi[:, slot, :], wraw[:, slot, :], ACT.Copy).then_inc(w_hi_made, 1)

            def split_ffn(ring, k):
                act.wait_ge(f_in_slot[ring.slot(k)], (ring.turn(k) + 1) * 16)
                act.activation(fhi[:, ring.slot(k), :], fraw[:, ring.slot(k), :], ACT.Copy).then_inc(f_hi_made, 1)

            def square(t, hn, before):
                act.activation(hn[:, t % 2, :], res[:, t, :], ACT.Square, scale=float(D) ** -0.5,
                               accum_out=ss[:, t:t + 1]).then_inc(squared, 1)
                act.wait_ge(squared, before + t + 1)
                rsqrt(rstd[:, t:t + 1], ss[:, t:t + 1], squared_log, before + t + 1, rstd_ready)

            def rsqrt(dst, src, logged, n, ready):
                act.activation(dst, src, ACT.Ln, bias=eps[:, 0:1]).then_inc(logged, 1)
                act.wait_ge(logged, n)
                act.activation(dst, dst, ACT.Exp, scale=-0.5).then_inc(ready, 1)

            def norm_hi(bank, t, c):
                act.activation(h_hi[:, 4 * c:4 * c + 4, t * P:(t + 1) * P],
                               bank.rearrange("p (k c) -> p k c", k=4), ACT.Copy).then_inc(acc_hi, 1)

            act.preload_act_table_set("natural_log_exp_and_others")
            act.wait_ge(consts, 3)
            def mlp(kind, i):
                ring = ffn_ring(i)
                accs = Accs("f", kind, i)

                def step(s):
                    if s[0] == "fsplit":
                        if s[1] >= 3:
                            before = ffn_tiles(kind)[s[1] - 3]
                            use = ("down", 2 * NT - 1) if before[0] == "d" else ("up", before[0], int(before[1]), 1, 3)
                            act.wait_ge(acc_full, accs.number(use))
                        else:
                            act.wait_ge(acc_full, accs.base if kind != "first" else MIX_ACC)
                        split_ffn(ring, s[1])
                    elif s[0] == "up" and s[-1] == 3:
                        _, what, a, hf, _ = s
                        col = i * 2 + (a + (FTILES if what == "v" else 0))
                        act.wait_ge(acc_full, accs.number(s))
                        if hf == 0 and not (kind == "first" and a == 0):
                            act.wait_ge(a_lo_done, i * 4 + 2 * a)
                        act.activation(ub[what][:, 2 + hf * HALF:2 + (hf + 1) * HALF], accs.of(s), ACT.Copy)
                        act.activation(half(z[what], hf), accs.of(s), ACT.Copy,
                                       scale=ffn_w[:, 2, bass.ds(col, 1)]).then_inc(u_ready, 1)
                    elif s[0] == "silu":
                        _, a, hf = s
                        act.wait_ge(acc_drained, accs.number(("up", "g", a, hf, 3)))
                        act.activation(half(z["g"], hf), half(z["g"], hf), ACT.Silu).then_inc(silu_done, 1)
                    elif s[0] == "prod":
                        _, a, hf = s
                        act.wait_ge(prod_done, i * 4 + (2 * a + hf + 1))
                        act.activation(half(a_hi[:, a, :], hf), half(z["g"], hf), ACT.Copy).then_inc(a_hi_done, 1)
                    elif s[0] == "fsquare":
                        t = s[1]
                        act.wait_ge(acc_drained, accs.number(("down", 2 * t + 1)))
                        if t >= 2:
                            act.wait_ge(stored[t % 2], 16 * (t // 2))
                        square(t, hn2, 2 * NT)

                return step

            def mixer(kind, j):
                steps = MIX[kind]
                accs, turns = Accs("m", kind, j), numbered(steps, TURN_KINDS)
                turn0 = mixer_base(TURN_KINDS, j)
                scores = numbered(steps, ("qk",))
                pvs = numbered(steps, ("pv",))
                mlp_step = mlp("first", 0) if kind == "last" else None
                before_norm, hn = (NT, hn2) if kind == "last" else (0, hn1)
                for s in steps:
                    if s[0] in MLP_STEPS:
                        mlp_step(s)
                    elif s[0] == "split":
                        split_mixer(kind, j, s[1])
                    elif s[0] == "proj" and s[3] == 3 and s[1] in "qk":
                        p, cols = accs.of(s), slice(s[2] * HALF, (s[2] + 1) * HALF)
                        act.wait_ge(acc_full, accs.number(s))
                        lo, up = slice(0, HD), slice(HD, P)
                        if s[1] == "q":
                            act.activation(Q[0][lo, cols], p[lo, :], ACT.Copy, scale=HD ** -0.5)
                            act.activation(Q[1][up, cols], p[up, :], ACT.Copy, scale=HD ** -0.5).then_inc(acc_hi, 1)
                        else:
                            act.activation(K1[0][lo, cols], p[lo, :], ACT.Copy)
                            act.activation(K2[0][up, cols], p[lo, :], ACT.Copy)
                            act.activation(K2[1][lo, cols], p[up, :], ACT.Copy)
                            act.activation(K1[1][up, cols], p[up, :], ACT.Copy).then_inc(acc_hi, 1)
                    elif s[0] == "proj" and s[3] == 3 and s[1:3] == ("u", 1):
                        if kind == "first":
                            act.wait_ge(consts, 7)
                        act.wait_ge(acc_drained, accs.number(s))
                        act.activation(y[:, :], cu[:, 2:2 + S], ACT.Copy,
                                       scale=now[:, 2:3]).then_inc(tap_ready, 1)
                    elif s[0] == "proj" and s[3] == 3 and s[1:3] == ("b", 1):
                        act.wait_ge(acc_drained, accs.number(s))
                        act.activation(cu[:, 2:2 + S], y[:, :], ACT.Square).then_inc(y_squared, 1)
                    elif s[0] == "vT":
                        n = turns[s]
                        act.wait_ge(turn_full, turn0 + (n + 1))
                        src = turn_of(turns, s).rearrange("p (t h d) -> p t h d", t=HT, h=2)
                        act.activation(V[:, HT * s[1]:HT * s[1] + HT, :, 0:HD], src, ACT.Copy).then_inc(turn_hi, 1)
                    elif s[0] == "attT":
                        n = turns[s]
                        act.wait_ge(now_ready, j + 1)
                        act.wait_ge(turn_full, turn0 + (n + 1))
                        act.activation(half(mixA_hi, s[1]), turn_of(turns, s), ACT.Copy,
                                       scale=now[:, 3:4]).then_inc(turn_hi, 1)
                    elif s[0] == "stat":
                        n = j * 2 + (s[1] + 1)
                        act.wait_ge(turn_full, turn0 + (turns[s] + 1))
                        rsqrt(cu[:, 2 + s[1] * HALF:2 + (s[1] + 1) * HALF], turn_of(turns, s), y_log, n, y_r_ready)
                    elif s[0] == "yhi":
                        act.wait_ge(turn_drained, turn0)
                        act.wait_ge(acc_full, accs.base)
                        act.activation(half(mixC_hi, s[1]), half(y, s[1]), ACT.Copy).then_inc(y_hi, 1)
                    elif s[0] == "exp":
                        _, hd, qb = s
                        act.wait_ge(logits_ready, j * (2 * NT) + (scores[("qk", hd, qb)] + 1))
                        n = P * (qb + 1)
                        sl = qb % 4
                        act.activation(prob[:, sl, 0:n], prob[:, sl, 0:n], ACT.Exp, bias=m_neg[:, sl:sl + 1],
                                       accum_out=l_sum[:, hd, qb:qb + 1]).then_inc(probs_ready, 1)
                    elif s[0] == "tp":
                        _, hd, g, p = s
                        n = turns[s]
                        slot_free = last_user(s, pvs)
                        if slot_free is not None:
                            act.wait_ge(pv_done, j * len(pvs) + (slot_free + 1))
                        act.wait_ge(turn_full, turn0 + (n + 1))
                        src = turn_of(turns, s).rearrange("p (k q) -> p k q", k=2)
                        if p < g:
                            act.activation(probT_hi[:, reg_slot(s), :, :], src, ACT.Copy).then_inc(turn_hi, 1)
                        else:
                            act.activation(diagT_hi[:, 0, :], src[:, 0, :], ACT.Copy)
                            act.activation(diagT_hi[:, 1, P:256], src[:, 1, P:256], ACT.Copy).then_inc(turn_hi, 1)
                    elif s[0] == "ocopy":
                        _, hd, g = s
                        act.wait_ge(pv_done, j * len(pvs) + (pvs[("pv", hd, g, g)] + 1))
                        act.activation(o_sb[:, 256 * g:256 * g + 256], pv_out[:, 0:256], ACT.Copy).then_inc(o_copied, 1)
                    elif s[0] == "oroot":
                        act.wait_ge(turn_drained, turn0 + (turns[("otok", s[1], 1)] + 1))
                        rsqrt(o_r[:, :], o_ss[:, :], o_log, j * 2 + (s[1] + 1), o_r_ready)
                    elif s[0] == "square":
                        t = s[1]
                        if kind == "first":
                            act.wait_ge(x_in[t], 16)
                        else:
                            act.wait_ge(acc_drained, accs.number(("out", 2 * t + 1)))
                        if t >= 2:
                            act.wait_ge(acc_full, accs.number(("nT", t - 2, 1)))
                        square(t, hn, before_norm)
                    elif s[0] == "nT":
                        act.wait_ge(acc_full, accs.number(s))
                        norm_hi(accs.of(s), s[1], s[2])

            mixer("first", 0)
            with act.Fori(1, NJ) as j:
                mixer("loop", j)
            mixer("last", NJ)

            with act.Fori(1, NI) as i:
                step = mlp("loop", i)
                for s in FFN["loop"]:
                    step(s)
            act.preload_act_table_set("natural_log_exp_and_others")
            step = mlp("last", NI)
            for s in FFN["last"]:
                step(s)

        @block.vector
        def _(dve):
            chain = {"base": 0, "n": 0}

            def then_chain(ins):
                chain["n"] += 1
                ins.then_inc(dve_chain, 1)
                dve.wait_ge(dve_chain, chain["base"] + chain["n"])

            def split_mixer(kind, j, k):
                slot = SLOTS[kind][k]
                dve.wait_ge(w_hi_made, tile_number(j, k))
                dve.tensor_tensor(wlo[:, slot, :], wraw[:, slot, :], whi[:, slot, :].bitcast(F32),
                                  ALU.subtract).then_inc(w_made, 1)

            def split_ffn(ring, k):
                dve.wait_ge(f_hi_made, ring.n(k) + 1)
                dve.tensor_tensor(flo[:, ring.slot(k), :], fraw[:, ring.slot(k), :],
                                  fhi[:, ring.slot(k), :].bitcast(F32), ALU.subtract).then_inc(f_made, 1)

            def scale(t, hn, row, before):
                dve.wait_ge(rstd_ready, before + t + 1)
                dve.scalar_tensor_tensor(out=hn[:, t % 2, :], in0=res[:, t, :], scalar=rstd[:, t:t + 1],
                                         in1=row[:, :], op0=ALU.mult, op1=ALU.mult).then_inc(scaled, 1)

            def norm_lo(bank, t, c):
                cols = slice(t * P, (t + 1) * P)
                dve.tensor_tensor(h_lo[:, 4 * c:4 * c + 4, cols], bank.rearrange("p (k c) -> p k c", k=4),
                                  h_hi[:, 4 * c:4 * c + 4, cols].bitcast(F32), ALU.subtract).then_inc(acc_drained, 1)

            def mlp(kind, i):
                ring = ffn_ring(i)
                accs = Accs("f", kind, i)
                ups = numbered(FFN[kind], ("up",))

                def step(s):
                    if s[0] == "fsplit":
                        split_ffn(ring, s[1])
                    elif s[0] == "pads":
                        dve.memset(ub["g"][:, 0:2], 0.0)
                        dve.memset(ub["v"][:, 0:2], 0.0).then_inc(pads, 1)
                        dve.wait_ge(pads, 1)
                    elif s[0] == "up" and s[-1] == 3:
                        _, what, a, hf, _ = s
                        zh = half(z[what], hf)
                        col = i * 2 + (a + (FTILES if what == "v" else 0))
                        dve.wait_ge(u_ready, i * 8 + (ups[key(s)] + 1))
                        then_chain(dve.scalar_tensor_tensor(
                            out=zh, in0=ub[what][:, 1 + hf * HALF:1 + (hf + 1) * HALF],
                            scalar=ffn_w[:, 1, bass.ds(col, 1)], in1=zh, op0=ALU.mult, op1=ALU.add))
                        dve.scalar_tensor_tensor(
                            out=zh, in0=ub[what][:, hf * HALF:(hf + 1) * HALF],
                            scalar=ffn_w[:, 0, bass.ds(col, 1)], in1=zh, op0=ALU.mult, op1=ALU.add).then_inc(acc_drained, 1)
                    elif s[0] == "prod":
                        _, a, hf = s
                        n = i * 4 + (2 * a + hf + 1)
                        zg, zv = half(z["g"], hf), half(z["v"], hf)
                        dve.wait_ge(silu_done, n)
                        dve.wait_ge(acc_drained, accs.number(("up", "v", a, hf, 3)))
                        dve.tensor_tensor(zg, zg, zv, ALU.mult).then_inc(prod_done, 1)
                        dve.wait_ge(a_hi_done, n)
                        dve.tensor_tensor(half(a_lo[:, a, :], hf), zg, half(a_hi[:, a, :], hf).bitcast(F32),
                                          ALU.subtract).then_inc(a_lo_done, 1)
                    elif s[0] == "down":
                        part = half(res[:, s[1] // 2, :], s[1] % 2)
                        dve.wait_ge(acc_full, accs.number(s))
                        dve.tensor_tensor(part, accs.of(s), part, ALU.add).then_inc(acc_drained, 1)
                    elif s[0] == "finish":
                        if s[1] == 0:
                            dve.wait_ge(gf_in, 16)
                        scale(s[1], hn2, gf_row, 2 * NT)

                return step

            def mixer(kind, j):
                steps = MIX[kind]
                accs, turns = Accs("m", kind, j), numbered(steps, TURN_KINDS)
                turn0 = mixer_base(TURN_KINDS, j)
                his = numbered(steps, TURN_HI_KINDS)
                hi0 = mixer_base(TURN_HI_KINDS, j)
                scores = numbered(steps, ("qk",))
                lo, up = slice(0, HD), slice(HD, P)

                def take_params():
                    if kind == "last":
                        dve.tensor_copy(now[:, 3:4], attn_g[:, j - 1:j]).then_inc(now_ready, 1)
                    else:
                        if kind == "loop":
                            dve.tensor_copy(now[:, 3:4], attn_g[:, bass.ds(j - 1, 1)])
                        dve.tensor_copy(now[:, 4:5], conv_g[:, bass.ds(j, 1)])
                        dve.tensor_copy(now[:, 0:3], mix_w[:, :, bass.ds(j, 1)].rearrange("p k a -> p (k a)"))\
                           .then_inc(now_ready, 1)
                    dve.wait_ge(now_ready, j + 1)

                if kind != "first":
                    dve.wait_ge(turn_drained, turn0)
                    take_params()
                mlp_step = mlp("first", 0) if kind == "last" else None
                before_norm, hn, row, row_in = (NT, hn2, g2_row, g2_in) if kind == "last" else (0, hn1, g1_row, g1_in)
                for s in steps:
                    if s[0] in MLP_STEPS:
                        mlp_step(s)
                    elif s[0] == "split":
                        split_mixer(kind, j, s[1])
                    elif s[0] == "params":
                        dve.wait_ge(params_turned, 1)
                        dve.tensor_copy(params[:, :], pv_out[:, 0:NCW + 5 * NJ]).then_inc(params_ready, 1)
                        dve.wait_ge(params_ready, 1)
                        dve.wait_ge(tables_in, 32)
                        dve.wait_ge(consts, 9)
                        take_params()
                    elif s[0] == "proj" and s[3] == 3:
                        p, cols = accs.of(s), slice(s[2] * HALF, (s[2] + 1) * HALF)
                        if s[1] in "qk":
                            dve.wait_ge(acc_hi, hi_number(kind, j, s))
                        else:
                            dve.wait_ge(acc_full, accs.number(s))
                        if s[1] == "q":
                            dve.scalar_tensor_tensor(out=Q[0][up, cols], in0=p[lo, :], scalar=HD ** -0.5,
                                                     in1=Q[0][lo, cols].bitcast(F32), op0=ALU.mult, op1=ALU.subtract)
                            dve.scalar_tensor_tensor(out=Q[1][lo, cols], in0=p[up, :], scalar=HD ** -0.5,
                                                     in1=Q[1][up, cols].bitcast(F32), op0=ALU.mult, op1=ALU.subtract)\
                               .then_inc(acc_drained, 1)
                        elif s[1] == "k":
                            dve.tensor_tensor(K1[0][up, cols], p[lo, :], K1[0][lo, cols].bitcast(F32), ALU.subtract)
                            dve.tensor_tensor(K2[0][lo, cols], p[lo, :], K1[0][lo, cols].bitcast(F32), ALU.subtract)
                            dve.tensor_tensor(K1[1][lo, cols], p[up, :], K1[1][up, cols].bitcast(F32), ALU.subtract)
                            dve.tensor_tensor(K2[1][up, cols], p[up, :], K1[1][up, cols].bitcast(F32), ALU.subtract)\
                               .then_inc(acc_drained, 1)
                        elif s[1] == "v":
                            dve.tensor_copy(o_sb[:, cols], p[:, :]).then_inc(acc_drained, 1)
                        elif s[1] == "c":
                            dve.tensor_copy(cu[:, 2 + s[2] * HALF:2 + (s[2] + 1) * HALF], p[:, :]).then_inc(acc_drained, 1)
                        elif s[1] == "u":
                            part = cu[:, 2 + s[2] * HALF:2 + (s[2] + 1) * HALF]
                            dve.wait_ge(acc_drained, accs.number(("proj", "c", 1, 3)))
                            dve.tensor_tensor(part, p[:, :], part, ALU.mult).then_inc(acc_drained, 1)
                        elif s[1] == "b":
                            if s[2] == 0:
                                dve.wait_ge(tap_ready, j + 1)
                                for tap in (1, 0):
                                    then_chain(dve.scalar_tensor_tensor(
                                        out=y[:, :], in0=cu[:, tap:tap + S], scalar=now[:, tap:tap + 1],
                                        in1=y[:, :], op0=ALU.mult, op1=ALU.add))
                            dve.tensor_tensor(y[:, cols], p[:, :], y[:, cols], ALU.mult).then_inc(acc_drained, 1)
                    elif s[0] == "vT":
                        dve.wait_ge(turn_hi, hi0 + (his[s] + 1))
                        src = turn_of(turns, s).rearrange("p (t h d) -> p t h d", t=HT, h=2)
                        vs = V[:, HT * s[1]:HT * s[1] + HT, :, :]
                        dve.tensor_tensor(vs[:, :, :, HD:P], src, vs[:, :, :, 0:HD].bitcast(F32),
                                          ALU.subtract).then_inc(turn_drained, 1)
                    elif s[0] == "attT":
                        dve.wait_ge(turn_hi, hi0 + (his[s] + 1))
                        dve.scalar_tensor_tensor(out=half(mixA_lo, s[1]), in0=turn_of(turns, s),
                                                 scalar=now[:, 3:4],
                                                 in1=half(mixA_hi, s[1]).bitcast(F32),
                                                 op0=ALU.mult, op1=ALU.subtract).then_inc(turn_drained, 1)
                    elif s[0] == "stat":
                        hf = s[1]
                        r = cu[:, 2 + hf * HALF:2 + (hf + 1) * HALF]
                        dve.wait_ge(y_r_ready, j * 2 + (hf + 1))
                        dve.scalar_tensor_tensor(out=half(y, hf), in0=half(y, hf), scalar=now[:, 4:5],
                                                 in1=r, op0=ALU.mult, op1=ALU.mult).then_inc(turn_drained, 1)
                    elif s[0] == "yhi":
                        hf = s[1]
                        dve.wait_ge(y_hi, (j - 1) * 2 + (hf + 1))
                        dve.tensor_tensor(half(mixC_lo, hf), half(y, hf), half(mixC_hi, hf).bitcast(F32),
                                          ALU.subtract).then_inc(y_lo, 1)
                    elif s[0] == "out":
                        part = half(res[:, s[1] // 2, :], s[1] % 2)
                        dve.wait_ge(acc_full, accs.number(s))
                        dve.tensor_tensor(part, accs.of(s), part, ALU.add).then_inc(acc_drained, 1)
                    elif s[0] == "logits":
                        _, hd, qb = s
                        n, sl = P * (qb + 1), qb % 4
                        dve.wait_ge(score_full, j * (2 * NT) + (scores[("qk", hd, qb)] + 1))
                        dve.memset(marker[:, 0:1], 0.0)
                        then_chain(dve.tensor_tensor_reduce(
                            prob[:, sl, 0:n], score[:, score_at(qb):score_at(qb) + n], bias[:, S - P - P * qb:S - P - P * qb + n], 1.0, -3e38,
                            ALU.add, ALU.max, m_raw[:, sl:sl + 1]))
                        dve.tensor_scalar(m_neg[:, sl:sl + 1], m_raw[:, sl:sl + 1], -1.0, None,
                                          ALU.mult).then_inc(logits_ready, 1)
                        if qb == NT - 1:
                            then_chain(dve.scalar_tensor_tensor(out=bias[:, :], in0=bias[:, :], scalar=0.5,
                                                                in1=half_log[:, :], op0=ALU.mult, op1=ALU.add))
                    elif s[0] == "tp":
                        _, hd, g, p = s
                        dve.wait_ge(turn_hi, hi0 + (his[s] + 1))
                        src = turn_of(turns, s).rearrange("p (k q) -> p k q", k=2)
                        if p < g:
                            dve.tensor_tensor(probT_lo[:, reg_slot(s), :, :], src,
                                              probT_hi[:, reg_slot(s), :, :].bitcast(F32),
                                              ALU.subtract).then_inc(turn_drained, 1)
                        else:
                            dve.tensor_tensor(diagT_lo[:, 0, :], src[:, 0, :], diagT_hi[:, 0, :].bitcast(F32),
                                              ALU.subtract)
                            dve.tensor_tensor(diagT_lo[:, 1, P:256], src[:, 1, P:256],
                                              diagT_hi[:, 1, P:256].bitcast(F32), ALU.subtract).then_inc(turn_drained, 1)
                    elif s[0] == "otok":
                        _, hd, hf = s
                        heads = att[:, :, hd * HD:(hd + 1) * HD]
                        dve.wait_ge(turn_full, turn0 + (turns[s] + 1))
                        src = turn_of(turns, s).rearrange("p (t c) -> p t c", t=HT)
                        part = heads[:, HT * hf:HT * hf + HT, :]
                        then_chain(dve.tensor_copy(part, src[:, :, 0:HD]))
                        whole = dve.tensor_tensor(part, part, src[:, :, HD:P], ALU.add)
                        if hf == 0:
                            whole.then_inc(turn_drained, 1)
                            continue
                        then_chain(whole)
                        then_chain(dve.reciprocal(l_inv[:, :], l_sum[:, hd, :]))
                        then_chain(dve.tensor_tensor(heads, heads,
                                                     l_inv[:, :].unsqueeze(2).to_broadcast([P, NT, HD]), ALU.mult))
                        squares = turn_of(turns, s).rearrange("p (t d) -> p t d", t=NT)
                        then_chain(dve.scalar_tensor_tensor(out=squares, in0=heads, scalar=1.0 / HD,
                                                            in1=heads, op0=ALU.mult, op1=ALU.mult))
                        dve.tensor_reduce(o_ss[:, :], squares, AX.X, ALU.add).then_inc(turn_drained, 1)
                    elif s[0] == "oscale":
                        hd = s[1]
                        dve.wait_ge(o_r_ready, j * 2 + (hd + 1))
                        heads = att[:, :, hd * HD:(hd + 1) * HD]
                        dve.tensor_tensor(heads, heads,
                                          o_r[:, :].unsqueeze(2).to_broadcast([P, NT, HD]), ALU.mult).then_inc(att_ready, 1)
                    elif s[0] == "scale":
                        if s[1] == 0:
                            dve.wait_ge(row_in, 16)
                        scale(s[1], hn, row, before_norm)
                    elif s[0] == "nT":
                        dve.wait_ge(acc_hi, hi_number(kind, j, s))
                        norm_lo(accs.of(s), s[1], s[2])

            mixer("first", 0)
            start = chain["n"]
            per = chained(MIX["loop"], NT)
            with dve.Fori(1, NJ) as j:
                chain.update(base=(j - 1) * per + start, n=0)
                mixer("loop", j)
                assert chain["n"] == per
            chain.update(base=start + (NJ - 1) * per, n=0)
            mixer("last", NJ)
            start = start + (NJ - 1) * per + chain["n"]
            with dve.Fori(1, NI) as i:
                chain.update(base=(i - 1) * 8 + start, n=0)
                step = mlp("loop", i)
                for s in FFN["loop"]:
                    step(s)
                assert chain["n"] == 8
            chain.update(base=start + (NI - 1) * 8, n=0)
            step = mlp("last", NI)
            for s in FFN["last"]:
                step(s)

        @block.tensor
        def _(pe):
            def product(p, lhs, rhs, first, last):
                (l_hi, l_lo), (r_hi, r_lo) = lhs, rhs
                pe.matmul(p, l_hi, r_hi, start=first, stop=False)
                pe.matmul(p, l_hi, r_lo, start=False, stop=False)
                return pe.matmul(p, l_lo, r_hi, start=False, stop=last)

            def turn_norm(bank, hn, t, c):
                for k in range(4):
                    ins = pe.transpose(bank[:, k * P:(k + 1) * P],
                                       hn[:, t % 2, (4 * c + k) * P:(4 * c + k + 1) * P], ident[:, :])
                ins.then_inc(acc_full, 1)

            def free_acc(accs, s):
                before = accs.before(s)
                if before is not None:
                    pe.wait_ge(acc_drained, before)

            pe.wait_ge(consts, 2)

            def mlp(kind, i):
                tiles = ffn_tiles(kind)
                ring = ffn_ring(i)
                accs = Accs("f", kind, i)

                def weights(tile):
                    sl = ring.slot(tiles.index(tile))
                    return fhi[:, sl, :], flo[:, sl, :]

                def step(s):
                    if s[0] == "up":
                        _, what, a, hf, c = s
                        tile = f"{what}{a}"
                        if c == 0:
                            free_acc(accs, s)
                            if kind == "first" and tile == "g0":
                                pe.wait_ge(acc_drained, accs.number(("nT", HT * (hf + 1) - 1, 1)))
                            if hf == 0:
                                pe.wait_ge(f_made, ring.n(tiles.index(tile)) + 1)
                        w_hi, w_lo = weights(tile)
                        for k in (2 * c, 2 * c + 1):
                            ins = product(accs.of(s), (w_hi[:, k * P:(k + 1) * P], w_lo[:, k * P:(k + 1) * P]),
                                          (half(h_hi[:, k, :], hf), half(h_lo[:, k, :], hf)), k == 0, k == KT - 1)
                        if c == 3:
                            ins.then_inc(acc_full, 1)
                    elif s[0] in ("downA", "down"):
                        t, hf = s[1] // 2, s[1] % 2
                        a, tile = (0, "dA") if s[0] == "downA" else (1, "dB")
                        use = ("down", s[1])
                        if a == 0:
                            free_acc(accs, use)
                        if s[1] == 0:
                            pe.wait_ge(f_made, ring.n(tiles.index(tile)) + 1)
                            pe.wait_ge(a_lo_done, i * 4 - 2 + 2 * a)
                        toks = slice(t * P, (t + 1) * P)
                        w = weights(tile)
                        ins = product(accs.of(use), (a_hi[:, a, toks], a_lo[:, a, toks]),
                                      (half(w[0], hf), half(w[1], hf)), a == 0, a == 1)
                        if a == 1:
                            ins.then_inc(acc_full, 1)

                return step

            def mixer(kind, j):
                steps = MIX[kind]
                tiles = mixer_tiles(kind)
                accs, turns = Accs("m", kind, j), numbered(steps, TURN_KINDS)
                turn0 = mixer_base(TURN_KINDS, j)
                scores = numbered(steps, ("qk",))
                groups = 0

                def weights(tile):
                    slot = SLOTS[kind][tiles.index(tile)]
                    return whi[:, slot, :], wlo[:, slot, :]

                def free_turn(s):
                    if not (kind == "first" and turns[s] < 2):
                        pe.wait_ge(turn_drained, turn0 + (turns[s] - 1))

                mlp_step = mlp("first", 0) if kind == "last" else None
                before_norm, hn = (NT, hn2) if kind == "last" else (0, hn1)
                for s in steps:
                    if s[0] in MLP_STEPS:
                        mlp_step(s)
                    elif s[0] == "params":
                        pe.wait_ge(rows_in, 64)
                        at = 0
                        for k in range(8):
                            rows = 2 * FTILES if k < 3 else NJ
                            ins = pe.transpose(pv_out[:, at:at + rows], param_rows[0:rows, k, :], ident[0:rows, 0:rows])
                            at += rows
                        ins.then_inc(params_turned, 1)
                        pe.wait_ge(consts, 6)
                    elif s[0] == "proj":
                        _, tile, hf, c = s
                        if c == 0:
                            free_acc(accs, s)
                            if kind == "first" and tile == "q":
                                pe.wait_ge(acc_drained, accs.number(("nT", HT * (hf + 1) - 1, 1)))
                            if hf == 0:
                                pe.wait_ge(w_made, tile_number(j, tiles.index(tile)))
                        w_hi, w_lo = weights(tile)
                        for k in (2 * c, 2 * c + 1):
                            ins = product(accs.of(s),
                                          (w_hi[:, k * P:(k + 1) * P], w_lo[:, k * P:(k + 1) * P]),
                                          (half(h_hi[:, k, :], hf), half(h_lo[:, k, :], hf)), k == 0, k == KT - 1)
                        if c == 3:
                            ins.then_inc(acc_full, 1)
                    elif s[0] == "vT":
                        hf = s[1]
                        free_turn(s)
                        pe.wait_ge(acc_drained, accs.number(("proj", "v", hf, 3)))
                        for t in range(HT):
                            ins = pe.transpose(turn_of(turns, s)[:, t * P:(t + 1) * P],
                                               o_sb[:, (HT * hf + t) * P:(HT * hf + t + 1) * P], ident[:, :])
                        ins.then_inc(turn_full, 1)
                    elif s[0] == "attT":
                        hf = s[1]
                        free_turn(s)
                        pe.wait_ge(att_ready, j * 2)
                        for t in range(HT):
                            ins = pe.transpose(turn_of(turns, s)[:, t * P:(t + 1) * P], att[:, HT * hf + t, :], ident[:, :])
                        ins.then_inc(turn_full, 1)
                    elif s[0] == "stat":
                        free_turn(s)
                        pe.wait_ge(y_squared, j + 1)
                        pe.matmul(turn_of(turns, s), mean64[:, :], cu[:, 2 + s[1] * HALF:2 + (s[1] + 1) * HALF],
                                  start=True, stop=True).then_inc(turn_full, 1)
                    elif s[0] in ("outC", "out"):
                        t, hf = s[1] // 2, s[1] % 2
                        use = ("out", s[1])
                        toks = slice(t * P, (t + 1) * P)
                        if s[0] == "outC":
                            free_acc(accs, use)
                            if s[1] == 0:
                                pe.wait_ge(w_made, tile_number(j, tiles.index("oC")))
                                pe.wait_ge(y_lo, j * 2)
                                if kind == "last":
                                    pe.wait_ge(o_copied, NJ * NT)
                                    pe.wait_ge(logits_ready, NJ * 2 * NT)
                            w = weights("oC")
                            product(accs.of(use), (mixC_hi[:, toks], mixC_lo[:, toks]),
                                    (half(w[0], hf), half(w[1], hf)), True, False)
                        else:
                            if s[1] == 0:
                                pe.wait_ge(w_made, tile_number(j, tiles.index("oA")))
                                pe.wait_ge(turn_drained, turn0 + (turns[("attT", 1)] + 1))
                            w = weights("oA")
                            product(accs.of(use), (mixA_hi[:, toks], mixA_lo[:, toks]),
                                    (half(w[0], hf), half(w[1], hf)), False, True).then_inc(acc_full, 1)
                    elif s[0] == "qk":
                        _, hd, qb = s
                        if scores[s] == 0:
                            pe.wait_ge(acc_drained, accs.number(("proj", "k", 1, 3)))
                        others = 1 if 1 <= qb < HT else 0
                        if not (kind == "first" and scores[s] <= others):
                            pe.wait_ge(logits_ready, j * (2 * NT) + (scores[s] - others))
                        q = Q[hd][:, qb * P:(qb + 1) * P]
                        for at, n in keys_of(qb):
                            to = score[:, score_at(qb) + at:score_at(qb) + at + n]
                            pe.matmul(to, q, K1[hd][:, at:at + n], start=True, stop=False)
                            ins = pe.matmul(to, q, K2[hd][:, at:at + n], start=False, stop=True)
                        ins.then_inc(score_full, 1)
                    elif s[0] == "tp":
                        _, hd, g, p = s
                        free_turn(s)
                        if p == 0:
                            pe.wait_ge(probs_ready, j * (2 * NT) + (hd * NT + 2 * g + 2))
                        for kb in range(2):
                            for q in range(2):
                                if p == g and kb == 1 and q == 0:
                                    continue
                                k = 2 * p + kb
                                ins = pe.transpose(turn_of(turns, s)[:, kb * 256 + q * P:kb * 256 + (q + 1) * P],
                                                   prob[:, 2 * (g % 2) + q, k * P:(k + 1) * P], ident[:, :])
                        ins.then_inc(turn_full, 1)
                    elif s[0] == "pv":
                        _, hd, g, p = s
                        pe.wait_ge(turn_drained, turn0 + (turns[("tp", hd, g, p)] + 1))
                        if p == 0 and not (kind == "first" and groups == 0):
                            pe.wait_ge(o_copied, j * NT + groups)
                        for kb in range(2):
                            k = 2 * p + kb
                            v = V[:, k, hd, :]
                            for n, part in enumerate((probT_hi, probT_lo) if p < g else (diagT_hi, diagT_lo)):
                                src = part[:, reg_slot(s), kb, :] if p < g else part[:, kb, :]
                                ins = pe.matmul(pv_out[:, 0:256], v, src, start=(k == 0 and n == 0),
                                                stop=(k == 2 * g + 1 and n == 1))
                        ins.then_inc(pv_done, 1)
                        if p == g:
                            groups += 1
                    elif s[0] == "otok":
                        _, hd, hf = s
                        free_turn(s)
                        pe.wait_ge(o_copied, j * NT + (hd * HT + 2 * (hf + 1)))
                        for t in range(HT):
                            ins = pe.transpose(turn_of(turns, s)[:, t * P:(t + 1) * P],
                                               o_sb[:, (HT * hf + t) * P:(HT * hf + t + 1) * P], ident[:, :])
                        ins.then_inc(turn_full, 1)
                    elif s[0] == "nT":
                        free_acc(accs, s)
                        pe.wait_ge(scaled, before_norm + s[1] + 1)
                        turn_norm(accs.of(s), hn, s[1], s[2])

            mixer("first", 0)
            with pe.Fori(1, NJ) as j:
                mixer("loop", j)
            mixer("last", NJ)

            with pe.Fori(1, NI) as i:
                step = mlp("loop", i)
                for s in FFN["loop"]:
                    step(s)
            step = mlp("last", NI)
            for s in FFN["last"]:
                step(s)


def bias_tables(S):
    import numpy as np
    dist = (S - P + np.arange(P)[:, None] - np.arange(S)[None, :]).astype(np.int64)
    seen = sum(((dist >= 0) & (dist <= window) & (dist % dilation == 0)).astype(np.int64)
               for window, dilation in ((128, 1), (512, 4), (2048, 16)))
    logs = np.where(seen > 0, np.log(np.maximum(seen, 1)), MASKED)
    first = np.where(seen > 0, -0.5 * dist + logs, MASKED)
    return first.astype(np.float32), (0.5 * logs).astype(np.float32)


_INS = ["x", "norm1_g", "w_in", "mix_conv_w", "attn_out_g", "conv_out_g", "w_out", "norm2_g", "ffn_up",
        "ffn_conv_w", "ffn_down", "final_norm_g"]


def kernel(**inputs):
    import numpy as np
    import concourse.bacc as bacc
    from concourse.bass_utils import run_bass_kernel_spmd

    nc = bacc.Bacc("TRN2", target_bir_lowering=False, num_devices=1, dynamic_dma_scratch_size=1024)
    arrays = {f"in_{n}": np.ascontiguousarray(inputs[n]) for n in _INS}
    arrays["in_bias"], arrays["in_logs"] = bias_tables(inputs["x"].shape[1])
    args = [nc.dram_tensor(n, a.shape, mybir.dt.from_np(a.dtype), kind="ExternalInput").ap() for n, a in arrays.items()]
    out = nc.dram_tensor("out", inputs["x"].shape, F32, kind="ExternalOutput").ap()
    build_program(nc, *args, out)
    r = run_bass_kernel_spmd(nc, [arrays], core_ids=[0])
    return r.results[0]["out"]
```

```python
from contextlib import ExitStack

import concourse.bass as bass
from concourse import mybir

F32 = mybir.dt.float32
F32R = mybir.dt.float32r
ALU = mybir.AluOpType
ACT = mybir.ActivationFunctionType
AX = mybir.AxisListType

P = 128
EPS = 1e-6
MASKED = -1e30


class Ring:

    def __init__(self, depth, turns, rest):
        self.depth, self.turns, self.rest = depth, turns, rest

    def n(self, k):
        return self.turns * self.depth + (self.rest + k)

    def slot(self, k):
        return (self.rest + k) % self.depth

    def turn(self, k):
        return self.turns + (self.rest + k) // self.depth


def mixer_tiles(kind):
    if kind == "first":
        return ["q", "k", "v", "c", "u", "b"]
    if kind == "last":
        return ["oC", "oA"]
    return ["q", "k", "v", "c", "u", "b", "oA", "oC"]


SLOTS = {"first": [0, 1, 2, 0, 2, 1, 2], "loop": [2, 0, 1, 0, 1, 2, 0, 1, 2], "last": [2, 0]}


def ffn_tiles(kind):
    if kind == "first":
        return ["g0", "v0", "g1", "v1"]
    if kind == "last":
        return ["dA", "dB"]
    return ["g0", "dA", "dB", "v0", "g1", "v1"]


def proj(tile, half):
    return [("proj", tile, half, c) for c in range(4)]


def up(what, a, half):
    return [("up", what, a, half, c) for c in range(4)]


ORDER = {
    "first": ["3vvvvqlqV.elVe", "qlqle.t.e", "qle..qtlp..ctp.e", "tqplt.cqplt.pee", "q.ttqlpcl.eetpt",
              "pq.lpo.eqlpcte.", ".o..ql.peqlt..rct.es", ".t.tqppcl..ptqpeleprs", "tcttptpppoc", "orsrs"],
    "loop": ["v3vvvqvlVvqvlev.e.V", ".tql.eq.l.pce", ".qle.tq..ltp.e", "qlpetc.qlt.etp..p", "qtqlpcte.lpt..et",
             "qp.qlplop.c.te.e.", "t.rpoql.c..sepqlt.e", "...qrpt.st.lctpp.qel.e.pc", "t.ttp.ot..p",
             "ppcrosrs"],
}
NORM_ORDER = "rnrrnnNNNrnNkNNrnNNkrNrnNxxxnNxNxrnxNNkxNxxxNxxxxxxxxxx"
BRIDGE_ORDER = "yTkTCmCCyCAAArCArACCnAAmnNCrCANCCnCrANANnNACrACANNNCmACrAnuruuAnNnrNuuNnNNuuuNuNNuu"


def ordered(order, queues):
    steps = []
    for token in order:
        steps += queues[token].pop(0)
    return steps


def first_norm_steps(NT):
    queues = {
        "r": [[("square", t)] for t in range(NT)],
        "n": [[("scale", t)] for t in range(NT)],
        "N": [[("nT", t, c)] for t in range(NT) for c in range(2)],
        "k": [[("split", n)] for n in range(3)],
        "x": [[c] for what, hf in ("q0", "k0", "v0", "q1", "k1") for c in proj(what, int(hf))],
    }
    queues["x"][12].insert(0, ("params",))
    steps = ordered(NORM_ORDER, queues)
    assert not any(queues.values())
    return steps


def mixer_steps(kind, NT):
    if kind == "first":
        steps = first_norm_steps(NT)
    else:
        tail = {1: [("yhi", 0), ("yhi", 1)], 3: [("split", 1)], 4: [("attT", 0)], 5: [("attT", 1)], 7: [("split", 2)]}
        steps = []
        for n, c in enumerate(proj("q", 0) + proj("q", 1) + proj("k", 0) + proj("k", 1)):
            steps += [c] + tail.get(n, [])
    fill = [[c] for x in "cub" for c in proj(x, 0) + proj(x, 1)]
    fill[3].append(("split", 4))
    fill[5].append(("split", 5))
    if kind != "first":
        fill[12].append(("split", 6))
        fill[20].append(("split", 7))
        fill += [[("outC", b), ("out", b)] for b in range(2 * NT)]
        fill[26].append(("stat", 0))
        fill[27].append(("stat", 1))
        fill[28].append(("split", 8))
    else:
        fill[20].append(("split", 6))
        fill += [[("stat", 0)], [("stat", 1)]]

    groups = [(hd, g) for hd in range(2) for g in range(NT // 2)]
    queues = {
        "v": [[c] for c in (proj("v", 0) if kind != "first" else []) + proj("v", 1)],
        "V": [[("vT", 0)], [("vT", 1)]],
        "3": [[("split", 3)]],
        "t": [[("tp", hd, g, p)] for hd, g in groups for p in range(g + 1)],
        "p": [[("pv", hd, g, p)] for hd, g in groups for p in range(g + 1)],
        "c": [[("ocopy", hd, g)] for hd, g in groups],
        "o": [[("otok", hd, hf)] for hd in range(2) for hf in range(2)],
        "r": [[("oroot", hd, hf)] for hd in range(2) for hf in range(2)],
        "s": [[("oscale", hd, hf)] for hd in range(2) for hf in range(2)],
        ".": fill,
    }
    for token, what in (("q", "qk"), ("l", "logits"), ("e", "exp")):
        queues[token] = [[(what, hd, qb)] for hd in range(2) for qb in range(NT)]
    for n, order in enumerate(ORDER[kind]):
        steps += ordered(order, queues)
        done = 2 * min(n + 1, len(groups))
        assert all(len(queues[token]) == 2 * len(groups) - done for token in "qle")
        assert len(queues["t"]) == sum(g + 1 for hd, g in groups[n:])
    assert not any(queue for token, queue in queues.items() if token != ".")
    for f in fill:
        steps += f
    return steps


def bridge_steps(NT):
    at = {t: i for i, t in enumerate(ffn_tiles("first"))}
    queues = {
        "y": [[("yhi", 0)], [("yhi", 1)]],
        "k": [[("split", 1)]],
        "T": [[("attT", 0)], [("attT", 1)]],
        "C": [[("outC", b)] for b in range(2 * NT)],
        "A": [[("out", b)] for b in range(2 * NT)],
        "m": [[("pads",), ("fsplit", 0)], [("fsplit", 1)], [("fsplit", 2)]],
        "r": [[("square", t)] for t in range(NT)],
        "n": [[("scale", t)] for t in range(NT)],
        "N": [[("nT", t, c)] for t in range(NT) for c in range(2)],
        "u": [[c] for c in up("g", 0, 0) + up("v", 0, 0) + up("g", 1, 0)[:3]],
    }
    steps = ordered(BRIDGE_ORDER, queues)
    assert not any(queues.values())
    steps += [("silu", 0, 0)] + up("g", 0, 1) + [("fsplit", at["g0"] + 3), ("prod", 0, 0), ("silu", 0, 1)]
    steps += up("v", 0, 1) + [("prod", 0, 1)]
    steps += up("g", 1, 0)[3:] + up("g", 1, 1) + [("fsplit", at["v0"] + 3), ("fsplit", at["g1"] + 3)]
    steps += [("silu", 1, 0), ("silu", 1, 1)]
    steps += up("v", 1, 0) + [("prod", 1, 0)] + up("v", 1, 1) + [("prod", 1, 1)]
    return steps


def ffn_steps(kind, NT):
    tiles = ffn_tiles(kind)
    at = {t: i for i, t in enumerate(tiles)}
    blocks = range(2 * NT)
    if kind == "last":
        early = 8
        steps = [("downA", b) for b in range(early)]
        for b in blocks:
            steps += ([("downA", b)] if b >= early else []) + [("down", b)]
            t = b // 2
            if b % 2 == 1:
                steps.append(("fsquare", t))
                if t >= 1:
                    steps.append(("finish", t - 1))
        return steps + [("finish", NT - 1)]
    downs = [s for b in blocks for s in (("downA", b), ("down", b))]
    steps = [("fsplit", 2)]
    for a in range(2):
        steps += up("g", a, 0) + up("g", a, 1) + [("fsplit", at[f"g{a}"] + 3)]
        if a == 0:
            steps += downs + [("fsplit", at["dA"] + 3), ("fsplit", at["dB"] + 3)]
        steps += [("silu", a, 0), ("silu", a, 1)]
        steps += up("v", a, 0) + [("prod", a, 0)] + up("v", a, 1) + [("prod", a, 1)]
        if a == 0:
            steps.append(("fsplit", at["v0"] + 3))
    return steps


CHUNKED = ("proj", "up")


def key(s):
    return s[:-1] if s[0] in CHUNKED else s


def opens(s):
    if s[0] in CHUNKED:
        return key(s) if s[-1] == 0 else None
    return {"outC": ("out",) + s[1:], "downA": ("down",) + s[1:], "nT": s}.get(s[0])


def numbered(steps, kinds):
    out = {}
    for s in steps:
        if s[0] in kinds and not (s[0] in CHUNKED and s[-1] != 3):
            out[key(s)] = len(out)
    return out


def plan_banks(steps, entry, tail):
    number = numbered(steps, ACC_KINDS)
    last, busy, plan = dict(entry), {}, {}
    for s in steps:
        use = opens(s)
        if use:
            free = [b for b in last if b not in busy]
            bank = min(free, key=lambda b: (-99 if last[b] is None else last[b], b))
            left = len(number) - len(plan)
            if left <= len(tail) and tail[-left] in free:
                bank = tail[-left]
            plan[use] = (bank, last[bank])
            busy[bank] = use
        if key(s) in number and not (s[0] in CHUNKED and s[-1] != 3):
            bank = plan[key(s)][0]
            last[bank] = number[key(s)]
            del busy[bank]
    assert not busy
    return plan, {b: n - len(number) for b, n in last.items()}


def no_later(left, entry):
    return all(left[b] <= entry[b] for b in left)


def reg_slot(s):
    _, hd, g, p = s
    return (hd * 6 + g * (g - 1) // 2 + p) % 2


def last_user(s, pvs):
    _, hd, g, p = s
    if p == g:
        return None
    order = [q for q in pvs if q[3] < q[2]]
    at = order.index(("pv", hd, g, p))
    return pvs[order[at - 2]] if at >= 2 else None


def chained(steps, NT):
    n = sum(s[0] == "logits" for s in steps)
    n += 5 * sum(s[0] == "otok" for s in steps)
    n += sum(s[0] == "logits" and s[2] == NT - 1 for s in steps)
    return n + 2 * sum(s[:3] == ("proj", "b", 0) and s[3] == 3 for s in steps)


ACC_KINDS = ("proj", "out", "nT", "up", "down")
TURN_KINDS = ("vT", "tp", "otok", "attT", "stat")
TURN_HI_KINDS = ("vT", "tp", "attT")
MLP_STEPS = ("up", "fsplit", "silu", "prod", "downA", "down", "fsquare", "finish", "pads")


def build_program(nc, x, norm1_g, w_in, mix_conv_w, attn_out_g, conv_out_g, w_out, norm2_g, ffn_up,
                  ffn_conv_w, ffn_down, final_norm_g, bias_table, log_counts, out):
    _, S, D = x.shape
    NT = S // P
    KT = D // P
    HALF = S // 2
    HT = NT // 2
    HD = 64
    D_ATTN = attn_out_g.shape[1]
    NJ = D_ATTN // P
    F = ffn_down.shape[1]
    FTILES = F // P
    NI = FTILES // 2
    assert D == 2 * D_ATTN and S == 1024 and FTILES % 2 == 0 and KT == 8

    bridge = bridge_steps(NT)
    MIX = {"first": mixer_steps("first", NT), "loop": mixer_steps("loop", NT), "last": bridge}
    FFN = {"first": bridge, "loop": ffn_steps("loop", NT), "last": ffn_steps("last", NT)}

    def total(steps, kinds):
        return len(numbered(steps, kinds))

    def mixer_base(kinds, j, before=0):
        if isinstance(j, int) and j == 0:
            return before
        first, loop = total(MIX["first"], kinds), total(MIX["loop"], kinds)
        return j * loop + (before + first - loop)

    def ffn_base(kinds, i, before=0):
        if isinstance(i, int) and i == 0:
            return before
        first, loop = total(bridge, kinds), total(FFN["loop"], kinds)
        return i * loop + (before + first - loop)

    def since_stat(kind):
        def after(steps):
            turns = numbered(steps, TURN_KINDS)
            return len(turns) - 1 - turns[("stat", 1)]
        return after(MIX["loop"]) if kind == "last" else min(after(MIX["first"]), after(MIX["loop"]))

    def hi_number(kind, j, s):
        def has_hi(t):
            return t[0] == "nT" or (t[0] == "proj" and t[1] in "qk" and t[3] == 3)
        before = sum(map(has_hi, MIX["first"])) - sum(map(has_hi, MIX["loop"]))
        base = 0 if kind == "first" else j * sum(map(has_hi, MIX["loop"])) + before
        own = [key(t) for t in MIX[kind] if has_hi(t)]
        return base + (own.index(key(s)) + 1)

    MIX_ACC = mixer_base(ACC_KINDS, NJ)
    MIX_ENTRY = {0: -4, 1: -1, 2: -2}
    FFN_ENTRY = {6: -8, 7: -7, 0: -4, 1: -4, 2: -4, 3: -3, 4: -2, 5: -1}
    MIX_TAIL, FFN_TAIL = [0, 1, 2, 1], [6, 7] + list(range(6))
    PLAN = {}
    PLAN["m_first"], left = plan_banks(MIX["first"], {b: None for b in range(3)}, MIX_TAIL)
    assert no_later(left, MIX_ENTRY), left
    PLAN["m_loop"], left = plan_banks(MIX["loop"], MIX_ENTRY, MIX_TAIL)
    assert no_later(left, MIX_ENTRY), left
    PLAN["bridge"], left = plan_banks(bridge, {**MIX_ENTRY, 3: None, 4: None, 5: None}, FFN_TAIL[2:])
    assert no_later(left, FFN_ENTRY), left
    PLAN["f_loop"], left = plan_banks(FFN["loop"], FFN_ENTRY, FFN_TAIL)
    assert no_later(left, FFN_ENTRY), left
    PLAN["f_last"], _ = plan_banks(FFN["last"], FFN_ENTRY, [])
    PLAN["m_last"] = PLAN["f_first"] = PLAN["bridge"]
    assert all(total(MIX[k], TURN_KINDS) % 2 == 0 for k in MIX)

    def tile_number(j, k):
        return k + 1 if isinstance(j, int) and j == 0 else j * 8 + (k - 1)

    def slot_loads(kind, j, k):
        slot = SLOTS[kind][k]
        first, loop = SLOTS["first"][:-1].count(slot), SLOTS["loop"][:-1].count(slot)
        own = SLOTS[kind][:k + 1].count(slot)
        return own if kind == "first" else j * loop + (first - loop + own)

    def ffn_ring(i):
        return Ring(3, 0, 0) if isinstance(i, int) and i == 0 else Ring(3, i * 2 - 1, 1)

    ctx = ExitStack()
    with ctx:
        def sb(name, shape, dt=F32, scope=ctx):
            return scope.enter_context(nc.sbuf_tensor(name, shape, dt))

        def sem(name):
            return ctx.enter_context(nc.semaphore(name))

        h_hi = sb("h_hi", [P, KT, S], F32R)
        h_lo = sb("h_lo", [P, KT, S], F32R)
        res = sb("res", [P, NT, D])
        ident = sb("ident", [P, P])
        mean64 = sb("mean64", [P, P])
        params = sb("params", [P, 3 * 2 * FTILES + 5 * NJ])
        ss = sb("ss", [P, NT])
        rstd = sb("rstd", [P, NT])
        eps = sb("eps", [P, 1])
        now = sb("now", [P, 5])
        NCW = 3 * 2 * FTILES
        ffn_w = params[:, 0:NCW].rearrange("p (k t) -> p k t", k=3)
        mix_w = params[:, NCW:NCW + 3 * NJ].rearrange("p (k t) -> p k t", k=3)
        attn_g = params[:, NCW + 3 * NJ:NCW + 4 * NJ]
        conv_g = params[:, NCW + 4 * NJ:NCW + 5 * NJ]

        with ExitStack() as scope:
            hn1 = sb("hn1", [P, 2, D], F32, scope)
            g1_row = sb("g1_row", [1, D], F32, scope)
            param_rows = sb("param_rows", [P, 8, P], F32, scope)
        with ExitStack() as scope:
            mixA_hi = sb("mixA_hi", [P, S], F32R, scope)
            mixA_lo = sb("mixA_lo", [P, S], F32R, scope)
            mixC_hi = sb("mixC_hi", [P, S], F32R, scope)
            mixC_lo = sb("mixC_lo", [P, S], F32R, scope)
            Q = [sb(f"Q{n}", [P, S], F32R, scope) for n in range(2)]
            K1 = [sb(f"K1_{n}", [P, S], F32R, scope) for n in range(2)]
            K2 = [sb(f"K2_{n}", [P, S], F32R, scope) for n in range(2)]
            V = sb("V", [P, NT, 2, P], F32R, scope)
            probT_hi = sb("probT_hi", [P, 2, 2, 256], F32R, scope)
            probT_lo = sb("probT_lo", [P, 2, 2, 256], F32R, scope)
            diagT_hi = sb("diagT_hi", [P, 2, 256], F32R, scope)
            diagT_lo = sb("diagT_lo", [P, 2, 256], F32R, scope)
            prob = sb("prob", [P, 4, S], F32, scope)
            bias = sb("bias", [P, S], F32, scope)
            half_log = sb("half_log", [P, S], F32, scope)
            o_sb = sb("o_sb", [P, S], F32, scope)
            m_raw = sb("m_raw", [P, 4], F32, scope)
            marker = sb("marker", [P, 1], F32, scope)
            m_neg = sb("m_neg", [P, 4], F32, scope)
            l_sum = sb("l_sum", [P, 2, NT], F32, scope)
            l_inv = sb("l_inv", [P, NT], F32, scope)
            o_ss = sb("o_ss", [P, NT], F32, scope)
            o_r = sb("o_r", [P, NT], F32, scope)
            att = sb("att", [P, NT, P], F32, scope)
            whi = sb("whi", [P, 3, 1024], F32R, scope)
            with ExitStack() as raw:
                wraw = sb("wraw", [P, 3, 1024], F32, raw)
            wlo = sb("wlo", [P, 3, 1024], F32R, scope)
            cu = sb("cu", [P, 2 + S], F32, scope)
            y = sb("y", [P, S], F32, scope)
            ones = sb("ones", [1, P], F32, scope)
        with ExitStack() as scope:
            gf_row = sb("gf_row", [P, D], F32, scope)
            sb("below_output_parts", [P, 3 * S], F32, scope)
            fraw = sb("fraw", [P, 3, 1024], F32, scope)
            g2_row = sb("g2_row", [P, D], F32, scope)
            hn2 = sb("hn2", [P, 2, D], F32, scope)
            fhi = sb("fhi", [P, 3, 1024], F32R, scope)
            flo = sb("flo", [P, 3, 1024], F32R, scope)
            ub = {n: sb(f"ub_{n}", [P, 2 + S], F32, scope) for n in "gv"}
            z = {n: sb(f"z_{n}", [P, S], F32, scope) for n in "gv"}
            a_hi = sb("a_hi", [P, 2, S], F32R, scope)
            a_lo = sb("a_lo", [P, 2, S], F32R, scope)

        turn = [ctx.enter_context(nc.psum_tensor(f"turn{n}", [P, 512], F32)) for n in range(2)]
        acc_banks = [ctx.enter_context(nc.psum_tensor(f"acc{n}", [P, 512], F32)) for n in range(3)]
        score = ctx.enter_context(nc.psum_tensor("score", [P, 1024], F32))
        pv_out = ctx.enter_context(nc.psum_tensor("pv_out", [P, 512], F32))
        banks = [t[:, :] for t in acc_banks] + [score[:, 0:512], score[:, 512:1024], pv_out[:, :], turn[0][:, :], turn[1][:, :]]

        def turn_of(turns, s):
            return turn[turns[s] % 2][:, :]

        class Accs:

            def __init__(self, phase, kind, n):
                steps = (MIX if phase == "m" else FFN)[kind]
                self.plan = PLAN[f"{phase}_{kind}"]
                self.own = numbered(steps, ACC_KINDS)
                self.base = mixer_base(ACC_KINDS, n) if phase == "m" else ffn_base(ACC_KINDS, n, MIX_ACC)

            def of(self, s):
                return banks[self.plan[key(s)][0]]

            def number(self, s):
                return self.base + (self.own[key(s)] + 1)

            def before(self, s):
                last = self.plan[key(s)][1]
                return None if last is None else self.base + (last + 1)

        x_in = [sem(f"x_in{t}") for t in range(NT)]
        tables_in = sem("tables_in")
        rows_in = sem("rows_in")
        g1_in, g2_in, gf_in = sem("g1_in"), sem("g2_in"), sem("gf_in")
        g1_ready = sem("g1_ready")
        w_in_slot = [sem(f"w_in_slot{n}") for n in range(3)]
        f_in_slot = [sem(f"f_in_slot{n}") for n in range(3)]
        consts = sem("consts")
        params_turned = sem("params_turned")
        params_ready = sem("params_ready")
        w_hi_made, w_made = sem("w_hi_made"), sem("w_made")
        f_hi_made, f_made = sem("f_hi_made"), sem("f_made")
        squared = sem("squared")
        squared_log = sem("squared_log")
        rstd_ready = sem("rstd_ready")
        o_log, o_r_ready = sem("o_log"), sem("o_r_ready")
        y_log, y_r_ready = sem("y_log"), sem("y_r_ready")
        scaled = sem("scaled")
        acc_full, acc_drained = sem("acc_full"), sem("acc_drained")
        acc_hi = sem("acc_hi")
        turn_full, turn_drained, turn_hi = sem("turn_full"), sem("turn_drained"), sem("turn_hi")
        score_full = sem("score_full")
        logits_ready = sem("logits_ready")
        probs_ready = sem("probs_ready")
        pv_done = sem("pv_done")
        o_copied = sem("o_copied")
        att_ready = sem("att_ready")
        tap_ready = sem("tap_ready")
        now_ready = sem("now_ready")
        y_squared, y_hi, y_lo = sem("y_squared"), sem("y_hi"), sem("y_lo")
        pads = sem("pads")
        u_ready = sem("u_ready")
        silu_done, prod_done, a_hi_done, a_lo_done = sem("silu_done"), sem("prod_done"), sem("a_hi_done"), sem("a_lo_done")
        dve_chain = sem("dve_chain")
        stored = sem("stored")

        x_d = x[0].rearrange("(t p) d -> t p d", p=P)
        out_d = out[0].rearrange("(t p) d -> t p d", p=P)
        w_in_d = w_in[0].rearrange("(k p) c -> p k c", p=P)
        up_d = ffn_up[0].rearrange("(k p) c -> p k c", p=P)
        IN_AT = {"q": 0, "k": D_ATTN, "v": 2 * D_ATTN, "b": 3 * D_ATTN, "c": 3 * D_ATTN + D_ATTN, "u": 5 * D_ATTN}

        def half(t, n):
            return t[:, n * HALF:(n + 1) * HALF]

        def keys_of(qb):
            n = P * (qb + 1)
            pieces = [(0, min(max(n, 256), 512))]
            if n > 512:
                pieces.append((512, max(n - 512, 256)))
            return pieces

        def score_at(qb):
            return 512 if qb in (1, 3) else 0

        block = ctx.enter_context(nc.Block())

        @block.sync
        def _(sp):
            def mixer_weights(kind, j, ks):
                slots = SLOTS[kind]
                accs = Accs("m", kind, j)
                for k in ks:
                    slot = slots[k]
                    earlier = [n for n in range(k) if slots[n] == slot]
                    if earlier:
                        before = mixer_tiles(kind)[earlier[-1]]
                        sp.wait_ge(acc_full, accs.number(("proj", before, 1, 3)))
                    elif kind != "first":
                        sp.wait_ge(acc_full, accs.base)
                    tile, step = (mixer_tiles(kind) + ["next"])[k], j
                    if tile == "next":
                        tile, step = ("oC" if isinstance(j, int) and j == NJ - 1 else "q"), j + 1
                    dst = wraw[:, slot, :]
                    if tile[0] == "o":
                        row = (step - 1) * P + (0 if tile == "oA" else D_ATTN)
                        src = w_out[0][bass.ds(row, P), :]
                    else:
                        src = w_in_d[:, :, bass.ds(step * P + IN_AT[tile], P)]
                        dst = dst.rearrange("p (k c) -> p k c", k=KT)
                    sp.dma_start(dst, src).then_inc(w_in_slot[slot], 16)

            def ffn_weights(kind, i):
                ring = ffn_ring(i)
                for k, tile in enumerate(ffn_tiles(kind)):
                    if not (kind == "first" and k < 3):
                        sp.wait_ge(f_made, ring.n(k) - 2)
                    dst = fraw[:, ring.slot(k), :]
                    if tile[0] == "d":
                        row = (i - 1) * (2 * P) + (0 if tile == "dA" else P)
                        src = ffn_down[0][bass.ds(row, P), :]
                    else:
                        col = i * (2 * P) + (int(tile[1]) * P + (F if tile[0] == "v" else 0))
                        src = up_d[:, :, bass.ds(col, P)]
                        dst = dst.rearrange("p (k c) -> p k c", k=KT)
                    sp.dma_start(dst, src).then_inc(f_in_slot[ring.slot(k)], 16)

            sp.dma_start(g1_row[:], norm1_g[0].unsqueeze(0)).then_inc(g1_in, 16)
            sp.dma_start(res[:, 0, :], x_d[0]).then_inc(x_in[0], 16)
            for t in range(1, HT):
                sp.dma_start(res[:, t, :], x_d[t]).then_inc(x_in[t], 16)
            mixer_weights("first", 0, range(3))
            for t in range(HT, NT):
                sp.dma_start(res[:, t, :], x_d[t]).then_inc(x_in[t], 16)
            sp.dma_start(param_rows[0:2 * FTILES, 0:3, :],
                         ffn_conv_w[0].rearrange("k (t p) -> t k p", p=P)).then_inc(rows_in, 16)
            sp.dma_start(param_rows[0:NJ, 3:6, :],
                         mix_conv_w[0].rearrange("k (t p) -> t k p", p=P)).then_inc(rows_in, 16)
            sp.dma_start(param_rows[0:NJ, 6, :], attn_out_g[0].rearrange("(t p) -> t p", p=P)).then_inc(rows_in, 16)
            sp.dma_start(param_rows[0:NJ, 7, :], conv_out_g[0].rearrange("(t p) -> t p", p=P)).then_inc(rows_in, 16)
            sp.dma_start(bias[:], bias_table).then_inc(tables_in, 16)
            sp.dma_start(half_log[:], log_counts).then_inc(tables_in, 16)
            mixer_weights("first", 0, range(3, 7))
            with sp.Fori(1, NJ - 1) as j:
                mixer_weights("loop", j, range(1, 9))
            mixer_weights("loop", NJ - 1, range(1, 9))
            mixer_weights("last", NJ, range(1, 2))
            sp.wait_ge(score_full, 2 * NT * NJ)
            sp.dma_start(g2_row[:], norm2_g[0].partition_broadcast(P)).then_inc(g2_in, 16)
            ffn_weights("first", 0)
            mixed = Accs("m", "last", NJ)
            sp.wait_ge(acc_full, mixed.number(("out", 2 * NT - 1)))
            sp.dma_start(gf_row[:], final_norm_g.partition_broadcast(P)).then_inc(gf_in, 16)
            with sp.Fori(1, NI) as i:
                ffn_weights("loop", i)
            ffn_weights("last", NI)
            for t in range(NT - 1):
                sp.wait_ge(scaled, 2 * NT + t + 1)
                sp.dma_start(out_d[t], res[:, t, :]).then_inc(stored, 16)
            for hf in range(2):
                sp.wait_ge(scaled, 3 * NT + hf)
                sp.dma_start(half(out_d[NT - 1], hf), half(res[:, NT - 1, :], hf)).then_inc(stored, 16)
            sp.wait_ge(stored, 16 * (NT + 1))

        @block.gpsimd
        def _(pool):
            pool.memset(ones[:], 1.0).then_inc(consts, 1)
            pool.wait_ge(consts, 1)
            pool.memset(ident[:], 0.0).then_inc(consts, 1)
            pool.wait_ge(consts, 2)
            pool.affine_select(out=ident[:], in_=ident[:], compare_op=ALU.not_equal, fill=1.0, base=0,
                               pattern=[[-1, P]], channel_multiplier=1).then_inc(consts, 1)
            pool.wait_ge(consts, 3)
            pool.memset(eps[:], EPS).then_inc(consts, 1)
            pool.wait_ge(consts, 4)
            pool.memset(mean64[:], 0.0).then_inc(consts, 1)
            pool.wait_ge(consts, 5)
            pool.memset(mean64[0:HD, 0:HD], 1.0 / HD).then_inc(consts, 1)
            pool.wait_ge(consts, 6)
            pool.memset(mean64[HD:P, HD:P], 1.0 / HD).then_inc(consts, 1)
            pool.wait_ge(consts, 7)
            pool.memset(cu[:, 0:2], 0.0).then_inc(consts, 1)
            pool.wait_ge(consts, 8)
            pool.memset(diagT_hi[:, 1, 0:P].bitcast(F32), 0.0).then_inc(consts, 1)
            pool.wait_ge(consts, 9)
            pool.memset(diagT_lo[:, 1, 0:P].bitcast(F32), 0.0).then_inc(consts, 1)

        @block.scalar
        def _(act):
            def split_mixer(kind, j, k):
                slot = SLOTS[kind][k]
                act.wait_ge(w_in_slot[slot], slot_loads(kind, j, k) * 16)
                act.activation(whi[:, slot, :], wraw[:, slot, :], ACT.Copy).then_inc(w_hi_made, 1)

            def split_ffn(ring, k):
                act.wait_ge(f_in_slot[ring.slot(k)], (ring.turn(k) + 1) * 16)
                act.activation(fhi[:, ring.slot(k), :], fraw[:, ring.slot(k), :], ACT.Copy).then_inc(f_hi_made, 1)

            def square(t, before):
                act.activation(cu[:, 2:2 + D], res[:, t, :], ACT.Square, scale=float(D) ** -0.5,
                               accum_out=ss[:, t:t + 1]).then_inc(squared, 1)
                act.wait_ge(squared, before + t + 1)
                rsqrt(rstd[:, t:t + 1], ss[:, t:t + 1], squared_log, before + t + 1, rstd_ready)

            def rsqrt(dst, src, logged, n, ready):
                act.activation(dst, src, ACT.Ln, bias=eps[:, 0:1]).then_inc(logged, 1)
                act.wait_ge(logged, n)
                act.activation(dst, dst, ACT.Exp, scale=-0.5).then_inc(ready, 1)

            def norm_hi(bank, t, c):
                act.activation(h_hi[:, 4 * c:4 * c + 4, t * P:(t + 1) * P],
                               bank.rearrange("p (k c) -> p k c", k=4), ACT.Copy).then_inc(acc_hi, 1)

            act.preload_act_table_set("natural_log_exp_and_others")
            act.wait_ge(consts, 4)
            def mlp(kind, i):
                ring = ffn_ring(i)
                accs = Accs("f", kind, i)

                def step(s):
                    if s[0] == "fsplit":
                        if s[1] >= 3:
                            before = ffn_tiles(kind)[s[1] - 3]
                            use = ("down", 2 * NT - 1) if before[0] == "d" else ("up", before[0], int(before[1]), 1, 3)
                            act.wait_ge(acc_full, accs.number(use))
                        else:
                            act.wait_ge(acc_full, accs.base if kind != "first" else MIX_ACC)
                        split_ffn(ring, s[1])
                    elif s[0] == "up" and s[-1] == 3:
                        _, what, a, hf, _ = s
                        col = i * 2 + (a + (FTILES if what == "v" else 0))
                        act.wait_ge(acc_full, accs.number(s))
                        if hf == 0 and not (kind == "first" and a == 0):
                            act.wait_ge(a_lo_done, i * 4 + 2 * a)
                        act.activation(ub[what][:, 2 + hf * HALF:2 + (hf + 1) * HALF], accs.of(s), ACT.Copy)
                        act.activation(half(z[what], hf), accs.of(s), ACT.Copy,
                                       scale=ffn_w[:, 2, bass.ds(col, 1)]).then_inc(u_ready, 1)
                    elif s[0] == "silu":
                        _, a, hf = s
                        act.wait_ge(acc_drained, accs.number(("up", "g", a, hf, 3)))
                        act.activation(half(z["g"], hf), half(z["g"], hf), ACT.Silu).then_inc(silu_done, 1)
                    elif s[0] == "prod":
                        _, a, hf = s
                        act.wait_ge(prod_done, i * 4 + (2 * a + hf + 1))
                        act.activation(half(a_hi[:, a, :], hf), half(z["g"], hf), ACT.Copy).then_inc(a_hi_done, 1)
                    elif s[0] == "fsquare":
                        t = s[1]
                        act.wait_ge(acc_drained, accs.number(("down", 2 * t + 1)))
                        square(t, 2 * NT)

                return step

            def mixer(kind, j):
                steps = MIX[kind]
                accs, turns = Accs("m", kind, j), numbered(steps, TURN_KINDS)
                turn0 = mixer_base(TURN_KINDS, j)
                scores = numbered(steps, ("qk",))
                pvs = numbered(steps, ("pv",))
                mlp_step = mlp("first", 0) if kind == "last" else None
                before_norm = NT if kind == "last" else 0
                for s in steps:
                    if s[0] in MLP_STEPS:
                        mlp_step(s)
                    elif s[0] == "split":
                        split_mixer(kind, j, s[1])
                    elif s[0] == "proj" and s[3] == 3 and s[1] in "qk":
                        p, cols = accs.of(s), slice(s[2] * HALF, (s[2] + 1) * HALF)
                        act.wait_ge(acc_full, accs.number(s))
                        lo, up = slice(0, HD), slice(HD, P)
                        if s[1] == "q":
                            act.activation(Q[0][lo, cols], p[lo, :], ACT.Copy, scale=HD ** -0.5)
                            act.activation(Q[1][up, cols], p[up, :], ACT.Copy, scale=HD ** -0.5).then_inc(acc_hi, 1)
                        else:
                            act.activation(K1[0][lo, cols], p[lo, :], ACT.Copy)
                            act.activation(K2[0][up, cols], p[lo, :], ACT.Copy)
                            act.activation(K2[1][lo, cols], p[up, :], ACT.Copy)
                            act.activation(K1[1][up, cols], p[up, :], ACT.Copy).then_inc(acc_hi, 1)
                    elif s[0] == "proj" and s[3] == 3 and s[1:3] == ("u", 1):
                        if kind == "first":
                            act.wait_ge(consts, 8)
                        act.wait_ge(acc_drained, accs.number(s))
                        act.activation(y[:, :], cu[:, 2:2 + S], ACT.Copy,
                                       scale=now[:, 2:3]).then_inc(tap_ready, 1)
                    elif s[0] == "proj" and s[3] == 3 and s[1:3] == ("b", 1):
                        act.wait_ge(acc_drained, accs.number(s))
                        act.activation(cu[:, 2:2 + S], y[:, :], ACT.Square).then_inc(y_squared, 1)
                    elif s[0] == "vT":
                        n = turns[s]
                        act.wait_ge(turn_full, turn0 + (n + 1))
                        src = turn_of(turns, s).rearrange("p (t h d) -> p t h d", t=HT, h=2)
                        act.activation(V[:, HT * s[1]:HT * s[1] + HT, :, 0:HD], src, ACT.Copy).then_inc(turn_hi, 1)
                    elif s[0] == "attT":
                        n = turns[s]
                        act.wait_ge(now_ready, j + 1)
                        act.wait_ge(turn_full, turn0 + (n + 1))
                        act.activation(half(mixA_hi, s[1]), turn_of(turns, s), ACT.Copy,
                                       scale=now[:, 3:4]).then_inc(turn_hi, 1)
                    elif s[0] == "stat":
                        n = j * 2 + (s[1] + 1)
                        act.wait_ge(turn_full, turn0 + (turns[s] + 1))
                        rsqrt(cu[:, 2 + s[1] * HALF:2 + (s[1] + 1) * HALF], turn_of(turns, s), y_log, n, y_r_ready)
                    elif s[0] == "yhi":
                        act.wait_ge(turn_drained, turn0 - since_stat(kind))
                        act.wait_ge(acc_full, accs.base)
                        act.activation(half(mixC_hi, s[1]), half(y, s[1]), ACT.Copy).then_inc(y_hi, 1)
                    elif s[0] == "exp":
                        _, hd, qb = s
                        act.wait_ge(logits_ready, j * (2 * NT) + (scores[("qk", hd, qb)] + 1))
                        n = P * (qb + 1)
                        sl = qb % 4
                        act.activation(prob[:, sl, 0:n], prob[:, sl, 0:n], ACT.Exp, bias=m_neg[:, sl:sl + 1],
                                       accum_out=l_sum[:, hd, qb:qb + 1]).then_inc(probs_ready, 1)
                    elif s[0] == "tp":
                        _, hd, g, p = s
                        n = turns[s]
                        slot_free = last_user(s, pvs)
                        if slot_free is not None:
                            act.wait_ge(pv_done, j * len(pvs) + (slot_free + 1))
                        act.wait_ge(turn_full, turn0 + (n + 1))
                        src = turn_of(turns, s).rearrange("p (k q) -> p k q", k=2)
                        if p < g:
                            act.activation(probT_hi[:, reg_slot(s), :, :], src, ACT.Copy).then_inc(turn_hi, 1)
                        else:
                            act.activation(diagT_hi[:, 0, :], src[:, 0, :], ACT.Copy)
                            act.activation(diagT_hi[:, 1, P:256], src[:, 1, P:256], ACT.Copy).then_inc(turn_hi, 1)
                    elif s[0] == "ocopy":
                        _, hd, g = s
                        act.wait_ge(pv_done, j * len(pvs) + (pvs[("pv", hd, g, g)] + 1))
                        act.activation(o_sb[:, 256 * g:256 * g + 256], pv_out[:, 0:256], ACT.Copy).then_inc(o_copied, 1)
                    elif s[0] == "oroot":
                        _, hd, hf = s
                        toks = slice(HT * hf, HT * hf + HT)
                        act.wait_ge(turn_drained, turn0 + (turns[("otok", hd, hf)] + 1))
                        rsqrt(o_r[:, toks], o_ss[:, toks], o_log, j * 4 + (2 * hd + hf + 1), o_r_ready)
                    elif s[0] == "square":
                        t = s[1]
                        if kind == "first":
                            act.wait_ge(x_in[t], 16)
                        else:
                            act.wait_ge(acc_drained, accs.number(("out", 2 * t + 1)))
                        square(t, before_norm)
                    elif s[0] == "nT":
                        act.wait_ge(acc_full, accs.number(s))
                        norm_hi(accs.of(s), s[1], s[2])

            mixer("first", 0)
            with act.Fori(1, NJ) as j:
                mixer("loop", j)
            mixer("last", NJ)

            with act.Fori(1, NI) as i:
                step = mlp("loop", i)
                for s in FFN["loop"]:
                    step(s)
            act.preload_act_table_set("natural_log_exp_and_others")
            step = mlp("last", NI)
            for s in FFN["last"]:
                step(s)

        @block.vector
        def _(dve):
            chain = {"base": 0, "n": 0}

            def then_chain(ins):
                chain["n"] += 1
                ins.then_inc(dve_chain, 1)
                dve.wait_ge(dve_chain, chain["base"] + chain["n"])

            def split_mixer(kind, j, k):
                slot = SLOTS[kind][k]
                dve.wait_ge(w_hi_made, tile_number(j, k))
                dve.tensor_tensor(wlo[:, slot, :], wraw[:, slot, :], whi[:, slot, :].bitcast(F32),
                                  ALU.subtract).then_inc(w_made, 1)

            def split_ffn(ring, k):
                dve.wait_ge(f_hi_made, ring.n(k) + 1)
                dve.tensor_tensor(flo[:, ring.slot(k), :], fraw[:, ring.slot(k), :],
                                  fhi[:, ring.slot(k), :].bitcast(F32), ALU.subtract).then_inc(f_made, 1)

            def scale(t, out, row, before):
                dve.wait_ge(rstd_ready, before + t + 1)
                dve.scalar_tensor_tensor(out=out, in0=res[:, t, :], scalar=rstd[:, t:t + 1],
                                         in1=row[:, :], op0=ALU.mult, op1=ALU.mult).then_inc(scaled, 1)

            def norm_lo(bank, t, c):
                cols = slice(t * P, (t + 1) * P)
                dve.tensor_tensor(h_lo[:, 4 * c:4 * c + 4, cols], bank.rearrange("p (k c) -> p k c", k=4),
                                  h_hi[:, 4 * c:4 * c + 4, cols].bitcast(F32), ALU.subtract).then_inc(acc_drained, 1)

            def mlp(kind, i):
                ring = ffn_ring(i)
                accs = Accs("f", kind, i)
                ups = numbered(FFN[kind], ("up",))

                def step(s):
                    if s[0] == "fsplit":
                        split_ffn(ring, s[1])
                    elif s[0] == "pads":
                        dve.memset(ub["g"][:, 0:2], 0.0)
                        dve.memset(ub["v"][:, 0:2], 0.0).then_inc(pads, 1)
                        dve.wait_ge(pads, 1)
                    elif s[0] == "up" and s[-1] == 3:
                        _, what, a, hf, _ = s
                        zh = half(z[what], hf)
                        col = i * 2 + (a + (FTILES if what == "v" else 0))
                        dve.wait_ge(u_ready, i * 8 + (ups[key(s)] + 1))
                        then_chain(dve.scalar_tensor_tensor(
                            out=zh, in0=ub[what][:, 1 + hf * HALF:1 + (hf + 1) * HALF],
                            scalar=ffn_w[:, 1, bass.ds(col, 1)], in1=zh, op0=ALU.mult, op1=ALU.add))
                        dve.scalar_tensor_tensor(
                            out=zh, in0=ub[what][:, hf * HALF:(hf + 1) * HALF],
                            scalar=ffn_w[:, 0, bass.ds(col, 1)], in1=zh, op0=ALU.mult, op1=ALU.add).then_inc(acc_drained, 1)
                    elif s[0] == "prod":
                        _, a, hf = s
                        n = i * 4 + (2 * a + hf + 1)
                        zg, zv = half(z["g"], hf), half(z["v"], hf)
                        dve.wait_ge(silu_done, n)
                        dve.wait_ge(acc_drained, accs.number(("up", "v", a, hf, 3)))
                        dve.tensor_tensor(zg, zg, zv, ALU.mult).then_inc(prod_done, 1)
                        dve.wait_ge(a_hi_done, n)
                        dve.tensor_tensor(half(a_lo[:, a, :], hf), zg, half(a_hi[:, a, :], hf).bitcast(F32),
                                          ALU.subtract).then_inc(a_lo_done, 1)
                    elif s[0] == "down":
                        part = half(res[:, s[1] // 2, :], s[1] % 2)
                        dve.wait_ge(acc_full, accs.number(s))
                        dve.tensor_tensor(part, accs.of(s), part, ALU.add).then_inc(acc_drained, 1)
                    elif s[0] == "finish":
                        if s[1] == 0:
                            dve.wait_ge(gf_in, 16)
                        t = s[1]
                        if t < NT - 1:
                            scale(t, res[:, t, :], gf_row, 2 * NT)
                            return
                        dve.wait_ge(rstd_ready, 3 * NT)
                        for hf in range(2):
                            part = half(res[:, t, :], hf)
                            dve.scalar_tensor_tensor(out=part, in0=part, scalar=rstd[:, t:t + 1],
                                                     in1=half(gf_row, hf), op0=ALU.mult, op1=ALU.mult).then_inc(scaled, 1)

                return step

            def mixer(kind, j):
                steps = MIX[kind]
                accs, turns = Accs("m", kind, j), numbered(steps, TURN_KINDS)
                turn0 = mixer_base(TURN_KINDS, j)
                his = numbered(steps, TURN_HI_KINDS)
                hi0 = mixer_base(TURN_HI_KINDS, j)
                scores = numbered(steps, ("qk",))
                lo, up = slice(0, HD), slice(HD, P)

                def take_params():
                    if kind == "last":
                        dve.tensor_copy(now[:, 3:4], attn_g[:, j - 1:j]).then_inc(now_ready, 1)
                    else:
                        if kind == "loop":
                            dve.tensor_copy(now[:, 3:4], attn_g[:, bass.ds(j - 1, 1)])
                        dve.tensor_copy(now[:, 4:5], conv_g[:, bass.ds(j, 1)])
                        dve.tensor_copy(now[:, 0:3], mix_w[:, :, bass.ds(j, 1)].rearrange("p k a -> p (k a)"))\
                           .then_inc(now_ready, 1)
                    dve.wait_ge(now_ready, j + 1)

                if kind != "first":
                    dve.wait_ge(turn_drained, turn0)
                    take_params()
                mlp_step = mlp("first", 0) if kind == "last" else None
                before_norm, hn, row, row_in = (NT, hn2, g2_row, g2_in) if kind == "last" else (0, hn1, score, g1_ready)
                for s in steps:
                    if s[0] in MLP_STEPS:
                        mlp_step(s)
                    elif s[0] == "split":
                        split_mixer(kind, j, s[1])
                    elif s[0] == "params":
                        dve.wait_ge(params_turned, 1)
                        dve.tensor_copy(params[:, :], pv_out[:, 0:NCW + 5 * NJ]).then_inc(params_ready, 1)
                        dve.wait_ge(params_ready, 1)
                        dve.wait_ge(tables_in, 32)
                        dve.wait_ge(consts, 10)
                        take_params()
                    elif s[0] == "proj" and s[3] == 3:
                        p, cols = accs.of(s), slice(s[2] * HALF, (s[2] + 1) * HALF)
                        if s[1] in "qk":
                            dve.wait_ge(acc_hi, hi_number(kind, j, s))
                        else:
                            dve.wait_ge(acc_full, accs.number(s))
                        if s[1] == "q":
                            dve.scalar_tensor_tensor(out=Q[0][up, cols], in0=p[lo, :], scalar=HD ** -0.5,
                                                     in1=Q[0][lo, cols].bitcast(F32), op0=ALU.mult, op1=ALU.subtract)
                            dve.scalar_tensor_tensor(out=Q[1][lo, cols], in0=p[up, :], scalar=HD ** -0.5,
                                                     in1=Q[1][up, cols].bitcast(F32), op0=ALU.mult, op1=ALU.subtract)\
                               .then_inc(acc_drained, 1)
                        elif s[1] == "k":
                            dve.tensor_tensor(K1[0][up, cols], p[lo, :], K1[0][lo, cols].bitcast(F32), ALU.subtract)
                            dve.tensor_tensor(K2[0][lo, cols], p[lo, :], K1[0][lo, cols].bitcast(F32), ALU.subtract)
                            dve.tensor_tensor(K1[1][lo, cols], p[up, :], K1[1][up, cols].bitcast(F32), ALU.subtract)
                            dve.tensor_tensor(K2[1][up, cols], p[up, :], K1[1][up, cols].bitcast(F32), ALU.subtract)\
                               .then_inc(acc_drained, 1)
                        elif s[1] == "v":
                            dve.tensor_copy(o_sb[:, cols], p[:, :]).then_inc(acc_drained, 1)
                        elif s[1] == "c":
                            dve.tensor_copy(cu[:, 2 + s[2] * HALF:2 + (s[2] + 1) * HALF], p[:, :]).then_inc(acc_drained, 1)
                        elif s[1] == "u":
                            part = cu[:, 2 + s[2] * HALF:2 + (s[2] + 1) * HALF]
                            dve.wait_ge(acc_drained, accs.number(("proj", "c", 1, 3)))
                            dve.tensor_tensor(part, p[:, :], part, ALU.mult).then_inc(acc_drained, 1)
                        elif s[1] == "b":
                            if s[2] == 0:
                                dve.wait_ge(tap_ready, j + 1)
                                for tap in (1, 0):
                                    then_chain(dve.scalar_tensor_tensor(
                                        out=y[:, :], in0=cu[:, tap:tap + S], scalar=now[:, tap:tap + 1],
                                        in1=y[:, :], op0=ALU.mult, op1=ALU.add))
                            dve.tensor_tensor(y[:, cols], p[:, :], y[:, cols], ALU.mult).then_inc(acc_drained, 1)
                    elif s[0] == "vT":
                        dve.wait_ge(turn_hi, hi0 + (his[s] + 1))
                        src = turn_of(turns, s).rearrange("p (t h d) -> p t h d", t=HT, h=2)
                        vs = V[:, HT * s[1]:HT * s[1] + HT, :, :]
                        dve.tensor_tensor(vs[:, :, :, HD:P], src, vs[:, :, :, 0:HD].bitcast(F32),
                                          ALU.subtract).then_inc(turn_drained, 1)
                    elif s[0] == "attT":
                        dve.wait_ge(turn_hi, hi0 + (his[s] + 1))
                        dve.scalar_tensor_tensor(out=half(mixA_lo, s[1]), in0=turn_of(turns, s),
                                                 scalar=now[:, 3:4],
                                                 in1=half(mixA_hi, s[1]).bitcast(F32),
                                                 op0=ALU.mult, op1=ALU.subtract).then_inc(turn_drained, 1)
                    elif s[0] == "stat":
                        hf = s[1]
                        r = cu[:, 2 + hf * HALF:2 + (hf + 1) * HALF]
                        dve.wait_ge(y_r_ready, j * 2 + (hf + 1))
                        dve.scalar_tensor_tensor(out=half(y, hf), in0=half(y, hf), scalar=now[:, 4:5],
                                                 in1=r, op0=ALU.mult, op1=ALU.mult).then_inc(turn_drained, 1)
                    elif s[0] == "yhi":
                        hf = s[1]
                        dve.wait_ge(y_hi, (j - 1) * 2 + (hf + 1))
                        dve.tensor_tensor(half(mixC_lo, hf), half(y, hf), half(mixC_hi, hf).bitcast(F32),
                                          ALU.subtract).then_inc(y_lo, 1)
                    elif s[0] == "out":
                        part = half(res[:, s[1] // 2, :], s[1] % 2)
                        dve.wait_ge(acc_full, accs.number(s))
                        dve.tensor_tensor(part, accs.of(s), part, ALU.add).then_inc(acc_drained, 1)
                    elif s[0] == "logits":
                        _, hd, qb = s
                        n, sl = P * (qb + 1), qb % 4
                        dve.wait_ge(score_full, j * (2 * NT) + (scores[("qk", hd, qb)] + 1))
                        dve.memset(marker[:, 0:1], 0.0)
                        then_chain(dve.tensor_tensor_reduce(
                            prob[:, sl, 0:n], score[:, score_at(qb):score_at(qb) + n], bias[:, S - P - P * qb:S - P - P * qb + n], 1.0, -3e38,
                            ALU.add, ALU.max, m_raw[:, sl:sl + 1]))
                        dve.tensor_scalar(m_neg[:, sl:sl + 1], m_raw[:, sl:sl + 1], -1.0, None,
                                          ALU.mult).then_inc(logits_ready, 1)
                        if qb == NT - 1:
                            then_chain(dve.scalar_tensor_tensor(out=bias[:, :], in0=bias[:, :], scalar=0.5,
                                                                in1=half_log[:, :], op0=ALU.mult, op1=ALU.add))
                    elif s[0] == "tp":
                        _, hd, g, p = s
                        dve.wait_ge(turn_hi, hi0 + (his[s] + 1))
                        src = turn_of(turns, s).rearrange("p (k q) -> p k q", k=2)
                        if p < g:
                            dve.tensor_tensor(probT_lo[:, reg_slot(s), :, :], src,
                                              probT_hi[:, reg_slot(s), :, :].bitcast(F32),
                                              ALU.subtract).then_inc(turn_drained, 1)
                        else:
                            dve.tensor_tensor(diagT_lo[:, 0, :], src[:, 0, :], diagT_hi[:, 0, :].bitcast(F32),
                                              ALU.subtract)
                            dve.tensor_tensor(diagT_lo[:, 1, P:256], src[:, 1, P:256],
                                              diagT_hi[:, 1, P:256].bitcast(F32), ALU.subtract).then_inc(turn_drained, 1)
                    elif s[0] == "otok":
                        _, hd, hf = s
                        toks = slice(HT * hf, HT * hf + HT)
                        part = att[:, toks, hd * HD:(hd + 1) * HD]
                        dve.wait_ge(turn_full, turn0 + (turns[s] + 1))
                        src = turn_of(turns, s).rearrange("p (t c) -> p t c", t=HT)
                        then_chain(dve.tensor_copy(part, src[:, :, 0:HD]))
                        then_chain(dve.tensor_tensor(part, part, src[:, :, HD:P], ALU.add))
                        then_chain(dve.reciprocal(l_inv[:, toks], l_sum[:, hd, toks]))
                        then_chain(dve.tensor_tensor(part, part,
                                                     l_inv[:, toks].unsqueeze(2).to_broadcast([P, HT, HD]), ALU.mult))
                        squares = turn_of(turns, s)[:, 0:HT * HD].rearrange("p (t d) -> p t d", t=HT)
                        then_chain(dve.scalar_tensor_tensor(out=squares, in0=part, scalar=1.0 / HD,
                                                            in1=part, op0=ALU.mult, op1=ALU.mult))
                        dve.tensor_reduce(o_ss[:, toks], squares, AX.X, ALU.add).then_inc(turn_drained, 1)
                    elif s[0] == "oscale":
                        _, hd, hf = s
                        toks = slice(HT * hf, HT * hf + HT)
                        dve.wait_ge(o_r_ready, j * 4 + (2 * hd + hf + 1))
                        part = att[:, toks, hd * HD:(hd + 1) * HD]
                        dve.tensor_tensor(part, part,
                                          o_r[:, toks].unsqueeze(2).to_broadcast([P, HT, HD]), ALU.mult).then_inc(att_ready, 1)
                    elif s[0] == "scale":
                        if s[1] == 0:
                            dve.wait_ge(row_in, 1 if kind == "first" else 16)
                        if s[1] >= 2:
                            dve.wait_ge(acc_full, accs.number(("nT", s[1] - 2, 1)))
                        scale(s[1], hn[:, s[1] % 2, :], row, before_norm)
                    elif s[0] == "nT":
                        dve.wait_ge(acc_hi, hi_number(kind, j, s))
                        norm_lo(accs.of(s), s[1], s[2])

            mixer("first", 0)
            start = chain["n"]
            per = chained(MIX["loop"], NT)
            with dve.Fori(1, NJ) as j:
                chain.update(base=(j - 1) * per + start, n=0)
                mixer("loop", j)
                assert chain["n"] == per
            chain.update(base=start + (NJ - 1) * per, n=0)
            mixer("last", NJ)
            start = start + (NJ - 1) * per + chain["n"]
            with dve.Fori(1, NI) as i:
                chain.update(base=(i - 1) * 8 + start, n=0)
                step = mlp("loop", i)
                for s in FFN["loop"]:
                    step(s)
                assert chain["n"] == 8
            chain.update(base=start + (NI - 1) * 8, n=0)
            step = mlp("last", NI)
            for s in FFN["last"]:
                step(s)

        @block.tensor
        def _(pe):
            def product(p, lhs, rhs, first, last):
                (l_hi, l_lo), (r_hi, r_lo) = lhs, rhs
                pe.matmul(p, l_hi, r_hi, start=first, stop=False)
                pe.matmul(p, l_hi, r_lo, start=False, stop=False)
                return pe.matmul(p, l_lo, r_hi, start=False, stop=last)

            def turn_norm(bank, hn, t, c):
                for k in range(4):
                    ins = pe.transpose(bank[:, k * P:(k + 1) * P],
                                       hn[:, t % 2, (4 * c + k) * P:(4 * c + k + 1) * P], ident[:, :])
                ins.then_inc(acc_full, 1)

            def free_acc(accs, s):
                before = accs.before(s)
                if before is not None:
                    pe.wait_ge(acc_drained, before)

            pe.wait_ge(consts, 1)
            pe.wait_ge(g1_in, 16)
            for hf in range(2):
                ins = pe.matmul(half(score, hf), ones[:, :], half(g1_row, hf), start=True, stop=True)
            ins.then_inc(g1_ready, 1)
            pe.wait_ge(consts, 3)

            def mlp(kind, i):
                tiles = ffn_tiles(kind)
                ring = ffn_ring(i)
                accs = Accs("f", kind, i)

                def weights(tile):
                    sl = ring.slot(tiles.index(tile))
                    return fhi[:, sl, :], flo[:, sl, :]

                def step(s):
                    if s[0] == "up":
                        _, what, a, hf, c = s
                        tile = f"{what}{a}"
                        if c == 0:
                            free_acc(accs, s)
                            if kind == "first" and tile == "g0":
                                pe.wait_ge(acc_drained, accs.number(("nT", HT * (hf + 1) - 1, 1)))
                            if hf == 0:
                                pe.wait_ge(f_made, ring.n(tiles.index(tile)) + 1)
                        w_hi, w_lo = weights(tile)
                        for k in (2 * c, 2 * c + 1):
                            ins = product(accs.of(s), (w_hi[:, k * P:(k + 1) * P], w_lo[:, k * P:(k + 1) * P]),
                                          (half(h_hi[:, k, :], hf), half(h_lo[:, k, :], hf)), k == 0, k == KT - 1)
                        if c == 3:
                            ins.then_inc(acc_full, 1)
                    elif s[0] in ("downA", "down"):
                        t, hf = s[1] // 2, s[1] % 2
                        a, tile = (0, "dA") if s[0] == "downA" else (1, "dB")
                        use = ("down", s[1])
                        if a == 0:
                            free_acc(accs, use)
                        if s[1] == 0:
                            pe.wait_ge(f_made, ring.n(tiles.index(tile)) + 1)
                            pe.wait_ge(a_lo_done, i * 4 - 2 + 2 * a)
                        toks = slice(t * P, (t + 1) * P)
                        w = weights(tile)
                        ins = product(accs.of(use), (a_hi[:, a, toks], a_lo[:, a, toks]),
                                      (half(w[0], hf), half(w[1], hf)), a == 0, a == 1)
                        if a == 1:
                            ins.then_inc(acc_full, 1)

                return step

            def mixer(kind, j):
                steps = MIX[kind]
                tiles = mixer_tiles(kind)
                accs, turns = Accs("m", kind, j), numbered(steps, TURN_KINDS)
                turn0 = mixer_base(TURN_KINDS, j)
                scores = numbered(steps, ("qk",))
                groups = 0

                def weights(tile):
                    slot = SLOTS[kind][tiles.index(tile)]
                    return whi[:, slot, :], wlo[:, slot, :]

                def free_turn(s):
                    if not (kind == "first" and turns[s] < 2):
                        pe.wait_ge(turn_drained, turn0 + (turns[s] - 1))

                mlp_step = mlp("first", 0) if kind == "last" else None
                before_norm, hn = (NT, hn2) if kind == "last" else (0, hn1)
                for s in steps:
                    if s[0] in MLP_STEPS:
                        mlp_step(s)
                    elif s[0] == "params":
                        pe.wait_ge(rows_in, 64)
                        at = 0
                        for k in range(8):
                            rows = 2 * FTILES if k < 3 else NJ
                            ins = pe.transpose(pv_out[:, at:at + rows], param_rows[0:rows, k, :], ident[0:rows, 0:rows])
                            at += rows
                        ins.then_inc(params_turned, 1)
                        pe.wait_ge(consts, 7)
                    elif s[0] == "proj":
                        _, tile, hf, c = s
                        if c == 0:
                            free_acc(accs, s)
                            if kind == "first" and tile == "q":
                                pe.wait_ge(acc_drained, accs.number(("nT", HT * (hf + 1) - 1, 1)))
                            if hf == 0:
                                pe.wait_ge(w_made, tile_number(j, tiles.index(tile)))
                        w_hi, w_lo = weights(tile)
                        for k in (2 * c, 2 * c + 1):
                            ins = product(accs.of(s),
                                          (w_hi[:, k * P:(k + 1) * P], w_lo[:, k * P:(k + 1) * P]),
                                          (half(h_hi[:, k, :], hf), half(h_lo[:, k, :], hf)), k == 0, k == KT - 1)
                        if c == 3:
                            ins.then_inc(acc_full, 1)
                    elif s[0] == "vT":
                        hf = s[1]
                        free_turn(s)
                        pe.wait_ge(acc_drained, accs.number(("proj", "v", hf, 3)))
                        for t in range(HT):
                            ins = pe.transpose(turn_of(turns, s)[:, t * P:(t + 1) * P],
                                               o_sb[:, (HT * hf + t) * P:(HT * hf + t + 1) * P], ident[:, :])
                        ins.then_inc(turn_full, 1)
                    elif s[0] == "attT":
                        hf = s[1]
                        free_turn(s)
                        pe.wait_ge(att_ready, j * 4 - 1 + hf)
                        for t in range(HT):
                            ins = pe.transpose(turn_of(turns, s)[:, t * P:(t + 1) * P], att[:, HT * hf + t, :], ident[:, :])
                        ins.then_inc(turn_full, 1)
                    elif s[0] == "stat":
                        free_turn(s)
                        pe.wait_ge(y_squared, j + 1)
                        pe.matmul(turn_of(turns, s), mean64[:, :], cu[:, 2 + s[1] * HALF:2 + (s[1] + 1) * HALF],
                                  start=True, stop=True).then_inc(turn_full, 1)
                    elif s[0] in ("outC", "out"):
                        t, hf = s[1] // 2, s[1] % 2
                        use = ("out", s[1])
                        toks = slice(t * P, (t + 1) * P)
                        if s[0] == "outC":
                            free_acc(accs, use)
                            if s[1] == 0:
                                pe.wait_ge(w_made, tile_number(j, tiles.index("oC")))
                                pe.wait_ge(y_lo, j * 2 - 1)
                                if kind == "last":
                                    pe.wait_ge(o_copied, NJ * NT)
                                    pe.wait_ge(logits_ready, NJ * 2 * NT)
                            elif s[1] == NT:
                                pe.wait_ge(y_lo, j * 2)
                            w = weights("oC")
                            product(accs.of(use), (mixC_hi[:, toks], mixC_lo[:, toks]),
                                    (half(w[0], hf), half(w[1], hf)), True, False)
                        else:
                            if s[1] == 0:
                                pe.wait_ge(w_made, tile_number(j, tiles.index("oA")))
                                pe.wait_ge(turn_drained, turn0 + (turns[("attT", 0)] + 1))
                            elif s[1] == NT:
                                pe.wait_ge(turn_drained, turn0 + (turns[("attT", 1)] + 1))
                            w = weights("oA")
                            product(accs.of(use), (mixA_hi[:, toks], mixA_lo[:, toks]),
                                    (half(w[0], hf), half(w[1], hf)), False, True).then_inc(acc_full, 1)
                    elif s[0] == "qk":
                        _, hd, qb = s
                        if scores[s] == 0:
                            pe.wait_ge(acc_drained, accs.number(("proj", "k", 1, 3)))
                        others = 1 if 1 <= qb < HT else 0
                        if not (kind == "first" and scores[s] <= others):
                            pe.wait_ge(logits_ready, j * (2 * NT) + (scores[s] - others))
                        q = Q[hd][:, qb * P:(qb + 1) * P]
                        for at, n in keys_of(qb):
                            to = score[:, score_at(qb) + at:score_at(qb) + at + n]
                            pe.matmul(to, q, K1[hd][:, at:at + n], start=True, stop=False)
                            ins = pe.matmul(to, q, K2[hd][:, at:at + n], start=False, stop=True)
                        ins.then_inc(score_full, 1)
                    elif s[0] == "tp":
                        _, hd, g, p = s
                        free_turn(s)
                        if p == 0:
                            pe.wait_ge(probs_ready, j * (2 * NT) + (hd * NT + 2 * g + 2))
                        for kb in range(2):
                            for q in range(2):
                                if p == g and kb == 1 and q == 0:
                                    continue
                                k = 2 * p + kb
                                ins = pe.transpose(turn_of(turns, s)[:, kb * 256 + q * P:kb * 256 + (q + 1) * P],
                                                   prob[:, 2 * (g % 2) + q, k * P:(k + 1) * P], ident[:, :])
                        ins.then_inc(turn_full, 1)
                    elif s[0] == "pv":
                        _, hd, g, p = s
                        pe.wait_ge(turn_drained, turn0 + (turns[("tp", hd, g, p)] + 1))
                        if p == 0 and not (kind == "first" and groups == 0):
                            pe.wait_ge(o_copied, j * NT + groups)
                        for kb in range(2):
                            k = 2 * p + kb
                            v = V[:, k, hd, :]
                            for n, part in enumerate((probT_hi, probT_lo) if p < g else (diagT_hi, diagT_lo)):
                                src = part[:, reg_slot(s), kb, :] if p < g else part[:, kb, :]
                                ins = pe.matmul(pv_out[:, 0:256], v, src, start=(k == 0 and n == 0),
                                                stop=(k == 2 * g + 1 and n == 1))
                        ins.then_inc(pv_done, 1)
                        if p == g:
                            groups += 1
                    elif s[0] == "otok":
                        _, hd, hf = s
                        free_turn(s)
                        pe.wait_ge(o_copied, j * NT + (hd * HT + 2 * (hf + 1)))
                        for t in range(HT):
                            ins = pe.transpose(turn_of(turns, s)[:, t * P:(t + 1) * P],
                                               o_sb[:, (HT * hf + t) * P:(HT * hf + t + 1) * P], ident[:, :])
                        ins.then_inc(turn_full, 1)
                    elif s[0] == "nT":
                        free_acc(accs, s)
                        pe.wait_ge(scaled, before_norm + s[1] + 1)
                        turn_norm(accs.of(s), hn, s[1], s[2])

            mixer("first", 0)
            with pe.Fori(1, NJ) as j:
                mixer("loop", j)
            mixer("last", NJ)

            with pe.Fori(1, NI) as i:
                step = mlp("loop", i)
                for s in FFN["loop"]:
                    step(s)
            step = mlp("last", NI)
            for s in FFN["last"]:
                step(s)


def bias_tables(S):
    import numpy as np
    dist = (S - P + np.arange(P)[:, None] - np.arange(S)[None, :]).astype(np.int64)
    seen = sum(((dist >= 0) & (dist <= window) & (dist % dilation == 0)).astype(np.int64)
               for window, dilation in ((128, 1), (512, 4), (2048, 16)))
    logs = np.where(seen > 0, np.log(np.maximum(seen, 1)), MASKED)
    first = np.where(seen > 0, -0.5 * dist + logs, MASKED)
    return first.astype(np.float32), (0.5 * logs).astype(np.float32)


_INS = ["x", "norm1_g", "w_in", "mix_conv_w", "attn_out_g", "conv_out_g", "w_out", "norm2_g", "ffn_up",
        "ffn_conv_w", "ffn_down", "final_norm_g"]


def kernel(**inputs):
    import numpy as np
    import concourse.bacc as bacc
    from concourse.bass_utils import run_bass_kernel_spmd

    nc = bacc.Bacc("TRN2", target_bir_lowering=False, num_devices=1, dynamic_dma_scratch_size=1024)
    arrays = {f"in_{n}": np.ascontiguousarray(inputs[n]) for n in _INS}
    arrays["in_bias"], arrays["in_logs"] = bias_tables(inputs["x"].shape[1])
    args = [nc.dram_tensor(n, a.shape, mybir.dt.from_np(a.dtype), kind="ExternalInput").ap() for n, a in arrays.items()]
    out = nc.dram_tensor("out", inputs["x"].shape, F32, kind="ExternalOutput").ap()
    build_program(nc, *args, out)
    r = run_bass_kernel_spmd(nc, [arrays], core_ids=[0])
    return r.results[0]["out"]
```
